# Optimizing a Trainium2 kernel written in Bass

```python
import math
import numpy as np
import jax
import jax.numpy as jnp
from jax import lax

D_MODEL = 1024
BATCH = 1
SEQ = 1024
DEPTH = 2
DEC_BATCH = 8
DEC_SEQ = 4
PAST_LEN = 2048
PAGE_SIZE = 128

N_EVEN = (DEPTH + 1) // 2
N_ODD = DEPTH // 2
DIL_CFG = ((128, 1), (512, 4), (2048, 16))
N_DIL = 3
H_A = 4
DH_A = 64
BLK_A = 128
H_B = 4
DH_B = 128
MLSTM_CHUNK = 128
H_C = 16
KVH_C = 2
G_C = H_C // KVH_C
DH_C = 64
CMP_STRIDE = 16
CMP_BLK = 2 * CMP_STRIDE
CMP_HID = 64
SLC_BLK = 64
N_SEL = 16
WIN_C = 512
QBLK_C = 128
D_FF = -(-8 * D_MODEL // (3 * 256)) * 256
ROPE_THETA = 10000.0
EPS = 1e-6
A_QW = N_DIL * H_A * DH_A
B_W = H_B * DH_B
IN_AB = 3 * A_QW + 3 * B_W + 2 * H_B + B_W
MIX_AB = H_A * DH_A + B_W
C_Q = H_C * DH_C
C_KV = 3 * 2 * KVH_C * DH_C
IN_C = C_Q + C_KV + 3 * H_C
F32 = jnp.float32

kernel_name = 'hybrid_dilated_mlstm_nsa_decoder_step'

def ein(spec, *ops):
    return jnp.einsum(spec, *ops, preferred_element_type=F32)

def rms_norm(x, g):
    xf = x.astype(F32)
    y = xf * lax.rsqrt(jnp.mean(xf * xf, axis=-1, keepdims=True) + EPS)
    return (y * g.astype(F32)).astype(x.dtype)

def rope(x, pos):
    half = x.shape[-1] // 2
    inv = 1.0 / (ROPE_THETA ** (jnp.arange(half, dtype=F32) / half))
    ang = pos.astype(F32)[:, None] * inv[None, :]
    ang = ang.reshape((ang.shape[0],) + (1,) * (x.ndim - 3) + (half,))
    cos, sin = jnp.cos(ang), jnp.sin(ang)
    xf = x.astype(F32)
    x1, x2 = xf[..., :half], xf[..., half:]
    return jnp.concatenate([x1 * cos - x2 * sin, x2 * cos + x1 * sin], axis=-1).astype(x.dtype)

def masked_softmax(s, mask):
    s = jnp.where(mask, s, -jnp.inf)
    m = jnp.max(s, axis=-1, keepdims=True)
    m = jnp.where(jnp.isfinite(m), m, 0.0)
    p = jnp.exp(s - m)
    return p / jnp.maximum(jnp.sum(p, axis=-1, keepdims=True), 1e-30)

def swiglu(x, wg, wu, wd):
    return (jax.nn.silu(x @ wg) * (x @ wu)) @ wd

def dilated_prompt(q, k, v, window, dil):
    B, S, H, dh = q.shape
    nback = window // dil
    span = dil * BLK_A
    Sp = -(-S // span) * span
    M = Sp // dil
    NB = M // BLK_A

    def sub(x):
        x = jnp.pad(x, ((0, 0), (0, Sp - S), (0, 0), (0, 0)))
        x = x.reshape(B, M, dil, H, dh).transpose(0, 2, 1, 3, 4)
        return x.reshape(B, dil, NB, BLK_A, H, dh)

    def band(x):
        prev = jnp.concatenate([jnp.zeros_like(x[:, :, :1]), x[:, :, :-1]], axis=2)
        return jnp.concatenate([prev, x], axis=3)

    qb = sub(q)
    kk, vv = band(sub(k)), band(sub(v))
    s = ein('bgnqhd,bgnkhd->bgnhqk', qb, kk) * (dh ** -0.5)
    qi = BLK_A + jnp.arange(BLK_A)
    ki = jnp.arange(2 * BLK_A)
    rel = qi[:, None] - ki[None, :]
    band_ok = (rel >= 0) & (rel <= nback)
    first_ok = (jnp.arange(NB)[:, None, None] > 0) | (ki[None, None, :] >= BLK_A)
    mask = (band_ok[None] & first_ok)[None, None, :, None]
    s = jnp.where(mask, s, -jnp.inf)
    m = jnp.max(s, axis=-1, keepdims=True)
    p = jnp.exp(s - m)
    l = jnp.sum(p, axis=-1, keepdims=True)
    o = ein('bgnhqk,bgnkhd->bgnhqd', p, vv) / l
    lse = (m + jnp.log(l))[..., 0]
    o = o.transpose(0, 2, 4, 1, 3, 5).reshape(B, Sp, H, dh)[:, :S]
    lse = lse.transpose(0, 2, 4, 1, 3).reshape(B, Sp, H)[:, :S]
    return o, lse

def dilated_sample(q, kx, vx, window, dil, n_buf):
    T = q.shape[1]
    nback = window // dil
    idx = n_buf + np.arange(T)[:, None] - dil * np.arange(nback + 1)[None, :]
    valid = jnp.asarray(idx >= 0)[None, :, None, :]
    idc = np.clip(idx, 0, None)
    kg, vg = kx[:, idc], vx[:, idc]
    s = ein('bthd,btjhd->bthj', q, kg) * (q.shape[-1] ** -0.5)
    s = jnp.where(valid, s, -jnp.inf)
    m = jnp.max(s, axis=-1, keepdims=True)
    p = jnp.exp(s - m)
    l = jnp.sum(p, axis=-1, keepdims=True)
    o = ein('bthj,btjhd->bthd', p, vg) / l
    return o, (m + jnp.log(l))[..., 0]

def combine_groups(outs, lses):
    w = jax.nn.softmax(jnp.stack(lses, axis=0), axis=0)
    return jnp.sum(w[..., None] * jnp.stack(outs, axis=0), axis=0)

def mlstm(q, k, v, ig, lf, C0, n0, m0, chunk):
    B, S, H, dh = q.shape
    NC = S // chunk
    L = chunk

    def chunks(x):
        x = x.astype(F32).reshape((B, NC, L) + x.shape[2:])
        return jnp.swapaxes(jnp.moveaxis(x, 1, 0), 2, 3)

    tri = jnp.tril(jnp.ones((L, L), dtype=bool))

    def step(carry, xs):
        C, n, m = carry
        qc, kc, vc, ic, fc = xs
        b = jnp.cumsum(fc, axis=-1)
        a = b + m[..., None]
        D = b[..., :, None] - b[..., None, :] + ic[..., None, :]
        D = jnp.where(tri, D, -jnp.inf)
        mt = jnp.maximum(a, jnp.max(D, axis=-1))
        Dw = jnp.exp(D - mt[..., None])
        iw = jnp.exp(a - mt)
        sc = jnp.einsum('bhtd,bhsd->bhts', qc, kc) * Dw
        num = iw[..., None] * jnp.einsum('bhed,bhtd->bhte', C, qc) + jnp.einsum('bhts,bhse->bhte', sc, vc)
        den = iw * jnp.einsum('bhd,bhtd->bht', n, qc) + jnp.sum(sc, axis=-1)
        h = num / jnp.maximum(jnp.abs(den), jnp.exp(-mt))[..., None]
        mL = mt[..., -1]
        wL = jnp.exp(b[..., -1:] - b + ic - mL[..., None])
        dec = jnp.exp(a[..., -1] - mL)
        C = dec[..., None, None] * C + jnp.einsum('bhs,bhse,bhsd->bhed', wL, vc, kc)
        n = dec[..., None] * n + jnp.einsum('bhs,bhsd->bhd', wL, kc)
        return (C, n, mL), h

    carry0 = (C0.astype(F32), n0.astype(F32), m0.astype(F32))
    (C, n, m), hs = lax.scan(step, carry0, (chunks(q), chunks(k), chunks(v), chunks(ig), chunks(lf)))
    hs = jnp.moveaxis(jnp.swapaxes(hs, 2, 3), 0, 1).reshape(B, S, H, dh)
    return hs, (C, n, m)

def ab_project(hn, w_in, b_if, pos):
    B, S, _ = hn.shape
    z = hn @ w_in
    cuts = np.cumsum([A_QW, A_QW, A_QW, B_W, B_W, B_W, H_B, H_B])
    qa, ka, va, qb, kb, vb, ig, fg, og = jnp.split(z, cuts, axis=-1)
    grp = lambda t: t.reshape(B, S, N_DIL, H_A, DH_A)
    hd = lambda t: t.reshape(B, S, H_B, DH_B)
    ig = ig.astype(F32) + b_if[0]
    lf = jax.nn.log_sigmoid(fg.astype(F32) + b_if[1])
    return (rope(grp(qa), pos), rope(grp(ka), pos), grp(va),
            hd(qb), hd(kb) * (DH_B ** -0.5), hd(vb), ig, lf, og)

def ab_merge(o_a, h_b, og, g_mn, w_out, dtype):
    B, S = o_a.shape[:2]
    hb = h_b * lax.rsqrt(jnp.mean(h_b * h_b, axis=-1, keepdims=True) + EPS)
    hb = (hb * g_mn.astype(F32).reshape(H_B, DH_B)).reshape(B, S, B_W) * jax.nn.sigmoid(og.astype(F32))
    cat = jnp.concatenate([o_a.reshape(B, S, H_A * DH_A), hb], axis=-1).astype(dtype)
    return cat @ w_out

def ab_prompt(hn, w_in, b_if, g_mn, w_out):
    B, S, _ = hn.shape
    pos = jnp.arange(S)
    qa, ka, va, qb, kb, vb, ig, lf, og = ab_project(hn, w_in, b_if, pos)
    outs, lses, bufs = [], [], []
    for gi, (win, dil) in enumerate(DIL_CFG):
        o, lse = dilated_prompt(qa[:, :, gi], ka[:, :, gi], va[:, :, gi], win, dil)
        outs.append(o)
        lses.append(lse)
        nb = min(win, S)
        bufs.append(jnp.stack([ka[:, S - nb:, gi], va[:, S - nb:, gi]], axis=2))
    o_a = combine_groups(outs, lses)
    C0 = jnp.zeros((B, H_B, DH_B, DH_B), F32)
    n0 = jnp.zeros((B, H_B, DH_B), F32)
    m0 = jnp.zeros((B, H_B), F32)
    h_b, st = mlstm(qb, kb, vb, ig, lf, C0, n0, m0, MLSTM_CHUNK)
    return ab_merge(o_a, h_b, og, g_mn, w_out, hn.dtype), bufs, st

def ab_sample(hn, bufs_in, C0, n0, m0, w_in, b_if, g_mn, w_out):
    B, T, _ = hn.shape
    pos = PAST_LEN + jnp.arange(T)
    qa, ka, va, qb, kb, vb, ig, lf, og = ab_project(hn, w_in, b_if, pos)
    outs, lses, bufs = [], [], []
    for gi, (win, dil) in enumerate(DIL_CFG):
        buf = bufs_in[gi]
        n_buf = buf.shape[1]
        new = jnp.stack([ka[:, :, gi], va[:, :, gi]], axis=2)
        ext = jnp.concatenate([buf.astype(new.dtype), new], axis=1)
        o, lse = dilated_sample(qa[:, :, gi], ext[:, :, 0], ext[:, :, 1], win, dil, n_buf)
        outs.append(o)
        lses.append(lse)
        bufs.append(ext[:, T:])
    o_a = combine_groups(outs, lses)
    h_b, st = mlstm(qb, kb, vb, ig, lf, C0, n0, m0, T)
    return ab_merge(o_a, h_b, og, g_mn, w_out, hn.dtype), bufs, st

def c_project(hn, w_in, pos):
    B, S, _ = hn.shape
    z = hn @ w_in
    q = z[..., :C_Q].reshape(B, S, KVH_C, G_C, DH_C)
    kv = z[..., C_Q:C_Q + C_KV].reshape(B, S, 3, 2, KVH_C, DH_C)
    gates = jax.nn.sigmoid(z[..., C_Q + C_KV:].astype(F32)).reshape(B, S, KVH_C, G_C, 3)
    kv_cmp = kv[:, :, 0]
    kv_sel = jnp.stack([rope(kv[:, :, 1, 0], pos), kv[:, :, 1, 1]], axis=2)
    kv_win = jnp.stack([rope(kv[:, :, 2, 0], pos), kv[:, :, 2, 1]], axis=2)
    return q, rope(q, pos), kv_cmp, kv_sel, kv_win, gates

def compress(x, w1, w2, pe):
    B, L = x.shape[:2]
    n_cmp = (L - CMP_BLK) // CMP_STRIDE + 1
    ch = x[:, :(n_cmp + 1) * CMP_STRIDE].reshape(B, n_cmp + 1, CMP_STRIDE, KVH_C, DH_C)
    hid = (ein('bcrhd,rde->bche', ch[:, :-1], w1[:CMP_STRIDE])
           + ein('bcrhd,rde->bche', ch[:, 1:], w1[CMP_STRIDE:])
           + ein('rd,rde->e', pe, w1))
    return ein('bche,ed->bchd', jax.nn.gelu(hid), w2)

def slc_importance(p_grp, n_slc):
    n_cmp = p_grp.shape[-1]
    ratio = SLC_BLK // CMP_STRIDE
    offs = np.arange(1 - CMP_BLK // CMP_STRIDE, ratio)
    idx = ratio * np.arange(n_slc)[:, None] + offs[None, :]
    ok = jnp.asarray((idx >= 0) & (idx < n_cmp))
    g = p_grp[..., np.clip(idx, 0, n_cmp - 1)]
    return jnp.sum(jnp.where(ok, g, 0.0), axis=-1)

def nsa_attend(q, q_rot, gates, t, kc, vc, cmp_end, gather_sel, kw, vw, kw_pos, n_slc):
    scale = DH_C ** -0.5
    B, Q = q.shape[:2]
    mc = (cmp_end[None, :] <= t[:, None])[None, :, None, None, :]
    p_cmp = masked_softmax(ein('bqhgd,bnhd->bqhgn', q, kc) * scale, mc)
    o_cmp = ein('bqhgn,bnhd->bqhgd', p_cmp, vc)
    imp = slc_importance(jnp.sum(p_cmp, axis=3), n_slc)
    j = jnp.arange(n_slc)[None, :]
    cur = (t // SLC_BLK)[:, None]
    forced = ((j == 0) | (j == cur) | (j == cur - 1))[None, :, None, :]
    causal = (j <= cur)[None, :, None, :]
    imp = jnp.where(forced, jnp.inf, jnp.where(causal, imp, -jnp.inf))
    val, idx = lax.top_k(imp, min(N_SEL, n_slc))
    ks, vs = gather_sel(idx)
    kpos = idx[..., None] * SLC_BLK + jnp.arange(SLC_BLK)
    ms = (val > -jnp.inf)[..., None] & (kpos <= t[None, :, None, None, None])
    nk = ks.shape[3] * SLC_BLK
    ks = ks.reshape(B, Q, KVH_C, nk, DH_C)
    vs = vs.reshape(B, Q, KVH_C, nk, DH_C)
    ms = ms.reshape(B, Q, KVH_C, 1, nk)
    o_sel = ein('bqhgk,bqhkd->bqhgd', masked_softmax(ein('bqhgd,bqhkd->bqhgk', q_rot, ks) * scale, ms), vs)
    dlt = t[:, None] - kw_pos[None, :]
    mw = ((kw_pos[None, :] >= 0) & (dlt >= 0) & (dlt < WIN_C))[None, :, None, None, :]
    o_win = ein('bqhgn,bnhd->bqhgd', masked_softmax(ein('bqhgd,bnhd->bqhgn', q_rot, kw) * scale, mw), vw)
    o = gates[..., 0:1] * o_cmp + gates[..., 1:2] * o_sel + gates[..., 2:3] * o_win
    return o.reshape(B, Q, H_C * DH_C)

def c_prompt(hn, w_in, cmp_w1, cmp_w2, cmp_pe, w_out):
    B, S, _ = hn.shape
    pos = jnp.arange(S)
    q, q_rot, kv_cmp, kv_sel, kv_win, gates = c_project(hn, w_in, pos)
    kc = compress(kv_cmp[:, :, 0], cmp_w1[0], cmp_w2[0], cmp_pe[0])
    vc = compress(kv_cmp[:, :, 1], cmp_w1[1], cmp_w2[1], cmp_pe[1])
    cmp_end = jnp.arange(kc.shape[1]) * CMP_STRIDE + CMP_BLK - 1
    n_slc = S // SLC_BLK
    ksb = kv_sel[:, :, 0].reshape(B, n_slc, SLC_BLK, KVH_C, DH_C).transpose(0, 3, 1, 2, 4)
    vsb = kv_sel[:, :, 1].reshape(B, n_slc, SLC_BLK, KVH_C, DH_C).transpose(0, 3, 1, 2, 4)
    bi = jnp.arange(B)[:, None, None, None]
    hi = jnp.arange(KVH_C)[None, None, :, None]

    def gather_sel(idx):
        return ksb[bi, hi, idx], vsb[bi, hi, idx]

    kwp = jnp.pad(kv_win, ((0, 0), (WIN_C, 0), (0, 0), (0, 0), (0, 0)))

    def block(i):
        s0 = i * QBLK_C
        sl = lambda a: lax.dynamic_slice_in_dim(a, s0, QBLK_C, axis=1)
        t = s0 + jnp.arange(QBLK_C)
        kwb = lax.dynamic_slice_in_dim(kwp, s0, WIN_C + QBLK_C, axis=1)
        kw_pos = s0 - WIN_C + jnp.arange(WIN_C + QBLK_C)
        return nsa_attend(sl(q), sl(q_rot), sl(gates), t, kc, vc, cmp_end, gather_sel,
                          kwb[:, :, 0], kwb[:, :, 1], kw_pos, n_slc)

    o = lax.map(block, jnp.arange(S // QBLK_C))
    o = o.transpose(1, 0, 2, 3).reshape(B, S, H_C * DH_C)
    nw = min(WIN_C, S)
    return o.astype(hn.dtype) @ w_out, kv_cmp, kv_sel, kv_win[:, S - nw:]

def c_sample(hn, cmp_pool, sel_pool, win_buf, page_table, w_in, cmp_w1, cmp_w2, cmp_pe, w_out):
    DB, T, _ = hn.shape
    pos = PAST_LEN + jnp.arange(T)
    q, q_rot, kv_cmp, kv_sel, kv_win, gates = c_project(hn, w_in, pos)
    n_pages = page_table.shape[1]
    past = n_pages * PAGE_SIZE
    past_cmp = cmp_pool[page_table].reshape(DB, past, 2, KVH_C, DH_C).astype(kv_cmp.dtype)
    full = jnp.concatenate([past_cmp, kv_cmp], axis=1)
    kc = compress(full[:, :, 0], cmp_w1[0], cmp_w2[0], cmp_pe[0])
    vc = compress(full[:, :, 1], cmp_w1[1], cmp_w2[1], cmp_pe[1])
    cmp_end = jnp.arange(kc.shape[1]) * CMP_STRIDE + CMP_BLK - 1
    n_past_blk = past // SLC_BLK
    n_new_blk = -(-T // SLC_BLK)
    new_blocks = jnp.pad(kv_sel, ((0, 0), (0, n_new_blk * SLC_BLK - T), (0, 0), (0, 0), (0, 0)))
    new_blocks = new_blocks.reshape(DB, n_new_blk, SLC_BLK, 2, KVH_C, DH_C).transpose(0, 4, 1, 2, 3, 5)
    bi = jnp.arange(DB)[:, None, None, None]
    hi = jnp.arange(KVH_C)[None, None, :, None]

    def gather_sel(idx):
        row0 = idx * SLC_BLK
        phys = page_table[bi, jnp.clip(row0 // PAGE_SIZE, 0, n_pages - 1)]
        rows = (row0 % PAGE_SIZE)[..., None] + jnp.arange(SLC_BLK)
        g_past = sel_pool[phys[..., None], rows, :, hi[..., None]]
        g_new = new_blocks[bi, hi, jnp.clip(idx - n_past_blk, 0, n_new_blk - 1)]
        g = jnp.where((idx >= n_past_blk)[..., None, None, None], g_new, g_past)
        return g[..., 0, :], g[..., 1, :]

    n_buf = win_buf.shape[1]
    ext = jnp.concatenate([win_buf.astype(kv_win.dtype), kv_win], axis=1)
    kw_pos = PAST_LEN - n_buf + jnp.arange(n_buf + T)
    o = nsa_attend(q, q_rot, gates, pos, kc, vc, cmp_end, gather_sel,
                   ext[:, :, 0], ext[:, :, 1], kw_pos, n_past_blk + n_new_blk)
    return o.astype(hn.dtype) @ w_out, kv_cmp, kv_sel, ext[:, T:]

def setup_inputs(seed: int = 0) -> dict:
    key = jax.random.key(seed)
    ks = jax.random.split(key, 32)
    nrm = lambda i, shape, scale=1.0: scale * jax.random.normal(ks[i], shape, F32)
    n_pages = PAST_LEN // PAGE_SIZE
    n_phys = (5 * DEC_BATCH * n_pages + 3) // 4
    inp = {}
    inp['x_prompt'] = nrm(0, (BATCH, SEQ, D_MODEL))
    inp['x_sample'] = nrm(1, (DEC_BATCH, DEC_SEQ, D_MODEL))
    for g, (win, _) in enumerate(DIL_CFG):
        inp['cache_a%d_kv' % g] = nrm(2 + g, (N_EVEN, DEC_BATCH, min(win, PAST_LEN), 2, H_A, DH_A))
    inp['state_b_C'] = nrm(5, (N_EVEN, DEC_BATCH, H_B, DH_B, DH_B), DH_B ** -0.5)
    inp['state_b_n'] = nrm(6, (N_EVEN, DEC_BATCH, H_B, DH_B), DH_B ** -0.5)
    inp['state_b_m'] = jax.random.uniform(ks[7], (N_EVEN, DEC_BATCH, H_B), F32, 0.0, 2.0)
    inp['cache_c_cmp_kv'] = nrm(8, (N_ODD, n_phys, PAGE_SIZE, 2, KVH_C, DH_C))
    inp['cache_c_sel_kv'] = nrm(9, (N_ODD, n_phys, PAGE_SIZE, 2, KVH_C, DH_C))
    inp['cache_c_win_kv'] = nrm(10, (N_ODD, DEC_BATCH, min(WIN_C, PAST_LEN), 2, KVH_C, DH_C))
    perm = jax.random.permutation(ks[11], n_phys)
    inp['page_table'] = perm[:DEC_BATCH * n_pages].reshape(DEC_BATCH, n_pages).astype(jnp.int32)
    inp['norm_g'] = 1.0 + nrm(12, (DEPTH, 2, D_MODEL), 0.02)
    inp['w_in_ab'] = nrm(13, (N_EVEN, D_MODEL, IN_AB), D_MODEL ** -0.5)
    inp['b_if'] = jnp.stack([nrm(14, (N_EVEN, H_B), 0.1),
                             3.0 + 3.0 * jax.random.uniform(ks[15], (N_EVEN, H_B), F32)], axis=1)
    inp['g_mlstm'] = 1.0 + nrm(16, (N_EVEN, B_W), 0.02)
    inp['w_out_ab'] = nrm(17, (N_EVEN, MIX_AB, D_MODEL), MIX_AB ** -0.5)
    inp['w_in_c'] = nrm(18, (N_ODD, D_MODEL, IN_C), D_MODEL ** -0.5)
    inp['cmp_w1'] = nrm(19, (N_ODD, 2, CMP_BLK, DH_C, CMP_HID), (CMP_BLK * DH_C) ** -0.5)
    inp['cmp_w2'] = nrm(20, (N_ODD, 2, CMP_HID, DH_C), CMP_HID ** -0.5)
    inp['cmp_pe'] = nrm(21, (N_ODD, 2, CMP_BLK, DH_C), 0.5)
    inp['w_out_c'] = nrm(22, (N_ODD, C_Q, D_MODEL), C_Q ** -0.5)
    inp['w_ffn_gate'] = nrm(23, (DEPTH, D_MODEL, D_FF), D_MODEL ** -0.5)
    inp['w_ffn_up'] = nrm(24, (DEPTH, D_MODEL, D_FF), D_MODEL ** -0.5)
    inp['w_ffn_down'] = nrm(25, (DEPTH, D_FF, D_MODEL), D_FF ** -0.5)
    inp['norm_final'] = 1.0 + nrm(26, (D_MODEL,), 0.02)
    return inp

def reference(x_prompt, x_sample, cache_a0_kv, cache_a1_kv, cache_a2_kv, state_b_C, state_b_n, state_b_m,
              cache_c_cmp_kv, cache_c_sel_kv, cache_c_win_kv, page_table, norm_g, w_in_ab, b_if, g_mlstm,
              w_out_ab, w_in_c, cmp_w1, cmp_w2, cmp_pe, w_out_c, w_ffn_gate, w_ffn_up, w_ffn_down, norm_final):
    hp, hs = x_prompt, x_sample
    a_p, a_s = [[], [], []], [[], [], []]
    bC_p, bC_s, bn_p, bn_s, bm_p, bm_s = [], [], [], [], [], []
    cc_p, cc_s, csl_p, csl_s, cw_p, cw_s = [], [], [], [], [], []
    for layer in range(DEPTH):
        hn_p = rms_norm(hp, norm_g[layer, 0])
        hn_s = rms_norm(hs, norm_g[layer, 0])
        if layer % 2 == 0:
            e = layer // 2
            yp, bufp, (Cp, n_p, m_p) = ab_prompt(hn_p, w_in_ab[e], b_if[e], g_mlstm[e], w_out_ab[e])
            ys, bufs, (Cs, n_s, m_s) = ab_sample(hn_s, (cache_a0_kv[e], cache_a1_kv[e], cache_a2_kv[e]),
                                                 state_b_C[e], state_b_n[e], state_b_m[e],
                                                 w_in_ab[e], b_if[e], g_mlstm[e], w_out_ab[e])
            for gi in range(N_DIL):
                a_p[gi].append(bufp[gi])
                a_s[gi].append(bufs[gi])
            bC_p.append(Cp); bC_s.append(Cs)
            bn_p.append(n_p); bn_s.append(n_s)
            bm_p.append(m_p); bm_s.append(m_s)
        else:
            o = layer // 2
            yp, ccp, cslp, cwp = c_prompt(hn_p, w_in_c[o], cmp_w1[o], cmp_w2[o], cmp_pe[o], w_out_c[o])
            ys, ccs, csls, cws = c_sample(hn_s, cache_c_cmp_kv[o], cache_c_sel_kv[o], cache_c_win_kv[o],
                                          page_table, w_in_c[o], cmp_w1[o], cmp_w2[o], cmp_pe[o], w_out_c[o])
            cc_p.append(ccp); cc_s.append(ccs)
            csl_p.append(cslp); csl_s.append(csls)
            cw_p.append(cwp); cw_s.append(cws)
        hp = hp + yp
        hs = hs + ys
        hp = hp + swiglu(rms_norm(hp, norm_g[layer, 1]), w_ffn_gate[layer], w_ffn_up[layer], w_ffn_down[layer])
        hs = hs + swiglu(rms_norm(hs, norm_g[layer, 1]), w_ffn_gate[layer], w_ffn_up[layer], w_ffn_down[layer])
    y_prompt = rms_norm(hp, norm_final)
    y_sample = rms_norm(hs, norm_final)
    st = lambda xs: jnp.stack(xs, axis=0)
    return (y_prompt, y_sample,
            st(a_p[0]), st(a_s[0]), st(a_p[1]), st(a_s[1]), st(a_p[2]), st(a_s[2]),
            st(bC_p), st(bC_s), st(bn_p), st(bn_s), st(bm_p), st(bm_s),
            st(cc_p), st(cc_s), st(csl_p), st(csl_s), st(cw_p), st(cw_s))


_drawn_inputs = setup_inputs


def setup_inputs(seed=0):
    import zlib

    import numpy as np

    out = dict(_drawn_inputs(seed))
    spreads = {}
    factors = {'g_mlstm': 16.391, 'norm_final': 7.851, 'cache_c_cmp_kv': 3.701, 'cache_c_sel_kv': 5.251}
    for name, (base, spread) in spreads.items():
        noise = np.random.default_rng([zlib.crc32(name.encode()), seed]).standard_normal(out[name].shape)
        drawn = base * np.exp(spread * noise) if base else spread * noise
        out[name] = jnp.asarray(drawn.astype(out[name].dtype))
    for name, factor in factors.items():
        out[name] = (out[name] * factor).astype(out[name].dtype)
    return out
```

```python
from contextlib import ExitStack

import numpy as np

import concourse.bass as bass
from concourse import mybir

F32 = mybir.dt.float32
I32 = mybir.dt.int32
FR = mybir.dt.float32r
ACT = mybir.ActivationFunctionType
ALU = mybir.AluOpType
AX = mybir.AxisListType

P = 128
D = 1024
KD = D // P
SEQ = 1024
DEC_B, DEC_T = 8, 4
NS = DEC_B * DEC_T
TOK = SEQ + NS
TILES = -(-TOK // P)
ROWS = TILES * P
PT = SEQ // P
PAST = 2048
PAGE = 128
EPS = 1e-6
NEG = -1e30

DIL = ((128, 1), (512, 4), (2048, 16))
GA, HA, DA = 3, 4, 64
AW = HA * DA
QA = GA * AW
HB, DB = 4, 128
BW = HB * DB
IN_AB = 3 * QA + 4 * BW + 2 * HB
MIX = AW + BW
OFF_KA, OFF_VA = QA, 2 * QA
OFF_QB = 3 * QA
OFF_KB, OFF_VB = OFF_QB + BW, OFF_QB + 2 * BW
OFF_IG = OFF_QB + 3 * BW
OFF_FG, OFF_OG = OFF_IG + HB, OFF_IG + 2 * HB

HC, KVH, GC, DC = 16, 2, 8, 64
CQ = HC * DC
KVW = KVH * DC
IN_C = CQ + 6 * KVW + 3 * HC
OFF_CMP, OFF_SEL, OFF_WIN = CQ, CQ + 2 * KVW, CQ + 4 * KVW
OFF_GATE = CQ + 6 * KVW
STRIDE, CBLK, CHID = 16, 32, 64
SBLK, NSEL, WIN = 64, 16, 512
NCMP_P = (SEQ - CBLK) // STRIDE + 1
NCMP_S = (PAST + DEC_T - CBLK) // STRIDE + 1
NSLC = PAST // SBLK + 1
F = 2816
KF = F // P


class Sems:
    used = []

    def __init__(self, nc, ctx, tag):
        self.nc, self.tag = nc, tag

    def one(self, name):
        handle = self.nc.alloc_semaphore(name=f"{self.tag}_{name}")
        Sems.used.append(handle)
        return handle

    def __call__(self, name, n=None):
        return self.one(name) if n is None else [self.one(f"{name}{k}") for k in range(n)]


def recycle(nc):
    nc.clear_and_free_semaphores(Sems.used)
    Sems.used.clear()
    nc.all_engine_barrier()


def load_constants(nc, tag, src, dst):
    with ExitStack() as ctx:
        loaded = Sems(nc, ctx, tag)("loaded")
        with nc.Block() as block:

            @block.sync
            def _(sp):
                for s, d in zip(src, dst):
                    sp.dma_start(d, s, allow_slow_non_contiguous=True).then_inc(loaded, 16)
                sp.wait_ge(loaded, 16 * len(src))


def norm_transpose(nc, tag, h, gain, ident, xT, lo, spare=None):
    SLOTS = 3
    with ExitStack() as ctx:
        sb = lambda n, s: ctx.enter_context(nc.sbuf_tensor(f"{tag}_{n}", s, F32))
        sem = Sems(nc, ctx, tag)
        if spare is None:
            spare = sb("spare", [P, 3 * SLOTS + 1, D])
        rows, xn = spare[:, 0:SLOTS, 0:D], spare[:, SLOTS:2 * SLOTS, 0:D]
        whole = spare[:, 2 * SLOTS:3 * SLOTS, 0:D].rearrange("p s (k c) -> p s k c", c=P)
        sq = spare[:, 3 * SLOTS, 0:D]
        ss = sb("ss", [P, SLOTS])
        sd = sb("sd", [P, SLOTS])
        rs = sb("rs", [P, SLOTS])
        eps = sb("eps", [P, 1])
        ps = ctx.enter_context(nc.psum_tensor(f"{tag}_ps", [P, SLOTS, KD, P], F32))
        row_loaded = sem("row_loaded", SLOTS)
        hi_ready, lo_done = sem("hi_ready"), sem("lo_done")
        eps_set, row_free, sd_ready = sem("eps_set"), sem("row_free"), sem("sd_ready")
        scaled, turned, ps_free = sem("scaled"), sem("turned"), sem("ps_free")
        with nc.Block() as block:

            @block.sync
            def _(sp):
                with sp.Fori(0, TILES // SLOTS) as i:
                    for j in range(SLOTS):
                        sp.wait_ge(row_free, i * SLOTS + j + 1)
                        sp.dma_start(rows[:, j, :], h[bass.ds((i * SLOTS + j) * P, P), :]).then_inc(row_loaded[j], 16)

            @block.scalar
            def _(act):
                act.wait_ge(eps_set, 1)
                with act.Fori(0, TILES // SLOTS) as i:
                    for j in range(SLOTS):
                        act.wait_ge(row_loaded[j], 16 * i + 16)
                        nc.scalar.activation(sq, rows[:, j, :], ACT.Square, accum_out=ss[:, j:j + 1])
                        nc.scalar.drain()
                        nc.scalar.activation(sd[:, j:j + 1], ss[:, j:j + 1], ACT.Sqrt, scale=1.0 / D,
                                             bias=eps[:, 0:1]).then_inc(sd_ready, 1)

            @block.vector
            def _(dve):
                nc.vector.memset(eps[:], EPS).then_inc(eps_set, 1)
                dve.sem_inc(row_free, SLOTS)
                dve.sem_inc(ps_free, SLOTS)
                with dve.Fori(0, TILES // SLOTS) as i:
                    for j in range(SLOTS):
                        t = i * SLOTS + j
                        dve.wait_ge(sd_ready, t + 1)
                        nc.vector.reciprocal(rs[:, j:j + 1], sd[:, j:j + 1])
                        nc.vector.drain()
                        nc.vector.tensor_scalar(xn[:, j, :], rows[:, j, :], rs[:, j:j + 1], None, ALU.mult).then_inc(scaled, 1)
                        nc.vector.drain().then_inc(row_free, 1)
                        dve.wait_ge(turned, t + 1)
                        wide = gain.unsqueeze(2).to_broadcast([P, KD, P])
                        nc.vector.tensor_tensor(xT[:, :, bass.ds(t * P, P)], ps[:, j], wide, ALU.mult)
                        dve.wait_ge(lo_done, t + 1)
                        nc.vector.tensor_tensor(whole[:, j], ps[:, j], wide, ALU.mult).then_inc(ps_free, 1)
                        nc.vector.drain().then_inc(hi_ready, 1)

            @block.gpsimd
            def _(pool):
                pool.sem_inc(lo_done, SLOTS)
                with pool.Fori(0, TILES // SLOTS) as i:
                    for j in range(SLOTS):
                        cols = bass.ds((i * SLOTS + j) * P, P)
                        pool.wait_ge(hi_ready, i * SLOTS + j + 1)
                        nc.gpsimd.tensor_tensor(lo[:, :, cols], whole[:, j], xT[:, :, cols].bitcast(F32), ALU.subtract)
                        nc.gpsimd.drain().then_inc(lo_done, 1)

            @block.tensor
            def _(pe):
                with pe.Fori(0, TILES // SLOTS) as i:
                    for j in range(SLOTS):
                        t = i * SLOTS + j
                        pe.wait_ge(scaled, t + 1)
                        pe.wait_ge(ps_free, t + 1)
                        for k in range(KD):
                            last = nc.tensor.transpose(ps[:, j, k, :], xn[:, j, k * P:(k + 1) * P], ident)
                        last.then_inc(turned, 1)


def project(nc, tag, xT, kc, w, out, n, resid=None, meanwhile=None, lo=None):
    chunks = w.shape[-1] // n
    WS, BANKS = 2, 6
    per = WS * TILES
    assert w.shape[-1] == chunks * n and chunks % WS == 0 and per % BANKS == 0 and n <= 512
    w_v = w.rearrange("(k p) n -> p k n", p=P)
    SPLIT = 2 if resid is None else 1
    credit = BANKS // SPLIT
    copies = lambda i, q: i * (per // SPLIT) + q // SPLIT + 1
    with ExitStack() as ctx:
        sb = lambda nm, s: ctx.enter_context(nc.sbuf_tensor(f"{tag}_{nm}", s, F32))
        sem = Sems(nc, ctx, tag)
        wt = sb("w", [P, WS, kc, n])
        if lo is not None:
            fr = lambda nm: ctx.enter_context(nc.sbuf_tensor(f"{tag}_{nm}", [P, WS, kc, n], FR))
            w_hi, w_lo, zero = fr("w_hi"), fr("w_lo"), sb("zero", [P, n])
        w_split = sem("w_split")
        ot = sb("o", [P, BANKS, n])
        rt = sb("r", [P, BANKS, n]) if resid is not None else None
        ps = ctx.enter_context(nc.psum_tensor(f"{tag}_ps", [P, BANKS, 512], F32))
        w_loaded, w_used = sem("w_loaded", WS), sem("w_used")
        summed, copied = sem("summed"), sem("copied", SPLIT)
        stored = sem("stored", BANKS)
        r_loaded = sem("r_loaded", BANKS) if resid is not None else None
        where = lambda i, q: (bass.ds((q % TILES) * P, P), bass.ds((i * WS + q // TILES) * n, n))
        with nc.Block() as block:

            def load_chunk(eng, i, c):
                eng.wait_ge(w_used, i * WS + c + 1)
                eng.dma_start(wt[:, c], w_v[:, :, bass.ds((i * WS + c) * n, n)]).then_inc(w_loaded[c], 16)

            if lo is not None:

                @block.gpsimd
                def _(pool):
                    nc.gpsimd.memset(zero[:], 0.0)
                    nc.gpsimd.drain()

                    def load(c, j):
                        pool.dma_start(wt[:, j], w_v[:, :, bass.ds(c * n, n)]).then_inc(w_loaded[j], 16)

                    def split(c, j):
                        pool.wait_ge(w_used, c + 1)
                        pool.wait_ge(w_loaded[j], 8 * (c - j) + 16)
                        nc.gpsimd.tensor_tensor(w_hi[:, j], wt[:, j], zero[:].unsqueeze(1).to_broadcast([P, kc, n]), ALU.subtract)
                        nc.gpsimd.drain()
                        nc.gpsimd.tensor_tensor(w_lo[:, j], wt[:, j], w_hi[:, j].bitcast(F32), ALU.subtract)
                        nc.gpsimd.drain().then_inc(w_split, 1)

                    overlapped(pool, chunks, load, split)
            elif resid is None:

                @block.gpsimd
                def _(pool):
                    with pool.Fori(0, chunks // WS) as i:
                        for c in range(WS):
                            load_chunk(pool, i, c)
            if resid is not None:

                @block.scalar
                def _(act):
                    with act.Fori(0, chunks // WS) as i:
                        for c in range(WS):
                            if lo is None:
                                load_chunk(act, i, c)
                            for q in range(c * TILES, (c + 1) * TILES):
                                b = q % BANKS
                                act.wait_ge(stored[b], 16 * (i * (per // BANKS) + q // BANKS) + 16)
                                act.dma_start(rt[:, b], resid[where(i, q)]).then_inc(r_loaded[b], 16)

            @block.tensor
            def _(pe):
                pe.sem_inc(w_used, WS)
                with pe.Fori(0, chunks // WS) as i:
                    for s in range(WS):
                        if lo is None:
                            pe.wait_ge(w_loaded[s], 16 * i + 16)
                            parts = [(xT, wt)]
                        else:
                            pe.wait_ge(w_split, i * WS + s + 1)
                            parts = [(xT, w_hi), (xT, w_lo), (lo, w_hi)]
                        for t in range(TILES):
                            q = s * TILES + t
                            pe.wait_ge(copied[q % SPLIT], copies(i, q))
                            for k in range(kc):
                                for m, (x, y) in enumerate(parts):
                                    last = nc.tensor.matmul(ps[:, q % BANKS, 0:n], x[:, k, t * P:(t + 1) * P], y[:, s, k, :],
                                                            start=(k == 0 and m == 0), stop=(k == kc - 1 and m == len(parts) - 1))
                            last.then_inc(summed, 1)
                        nc.tensor.drain().then_inc(w_used, 1)

            def copy_out(eng, i, q):
                b = q % BANKS
                eng.wait_ge(summed, i * per + q + 1)
                eng.wait_ge(stored[b], 16 * (i * (per // BANKS) + q // BANKS) + 16)
                if resid is not None:
                    eng.wait_ge(r_loaded[b], 16 * (i * (per // BANKS) + q // BANKS) + 16)

            if resid is None:

                @block.scalar
                def _(act):
                    act.sem_inc(copied[0], credit)
                    with act.Fori(0, chunks // WS) as i:
                        for q in range(0, per, 2):
                            if meanwhile is not None and q == TILES - 1:
                                meanwhile(act, i)
                            copy_out(act, i, q)
                            nc.scalar.activation(ot[:, q % BANKS], ps[:, q % BANKS, 0:n], ACT.Copy).then_inc(copied[0], 1)

            @block.vector
            def _(dve):
                dve.sem_inc(copied[SPLIT - 1], credit)
                with dve.Fori(0, chunks // WS) as i:
                    for q in range(SPLIT - 1, per, SPLIT):
                        copy_out(dve, i, q)
                        b = q % BANKS
                        if resid is None:
                            nc.vector.tensor_copy(ot[:, b], ps[:, b, 0:n]).then_inc(copied[1], 1)
                        else:
                            nc.vector.tensor_tensor(ot[:, b], ps[:, b, 0:n], rt[:, b], ALU.add).then_inc(copied[0], 1)

            @block.sync
            def _(sp):
                for b in range(BANKS):
                    sp.sem_inc(stored[b], 16)
                with sp.Fori(0, chunks // WS) as i:
                    for q in range(per):
                        sp.wait_ge(copied[q % SPLIT], copies(i, q) + credit)
                        sp.dma_start(out[where(i, q)], ot[:, q % BANKS]).then_inc(stored[q % BANKS], 16)
                for b in range(BANKS):
                    sp.wait_ge(stored[b], 16 * (chunks // WS) * (per // BANKS) + 16)


def ffn_hidden(nc, tag, xT, lo, wg, wu, hT):
    WS, G = 2, 3
    N = TOK // G
    assert KF % WS == 0 and N * G == TOK and N <= 512 and N % 2 == 0 and (WS * G) % 2 == 0
    w_v = [w.rearrange("(k p) f -> p k f", p=P) for w in (wg, wu)]
    with ExitStack() as ctx:
        sb = lambda nm, s, t=F32: ctx.enter_context(nc.sbuf_tensor(f"{tag}_{nm}", s, t))
        sem = Sems(nc, ctx, tag)
        wt = sb("w", [P, D])
        w_hi, w_lo = sb("w_hi", [P, 2, KD, P], FR), sb("w_lo", [P, 2, KD, P], FR)
        zero = sb("zero", [P, 1])
        e = sb("e", [P, 2, N])
        ps = ctx.enter_context(nc.psum_tensor(f"{tag}_ps", [P, G, 2, 512], F32))
        w_loaded, w_split, w_used = sem("w_loaded"), sem("w_split"), sem("w_used")
        gate_done, up_done, e_ready, gated, used = (sem(n) for n in ("gate_done", "up_done", "e_ready", "gated", "used"))
        with nc.Block() as block:

            @block.sync
            def _(sp):
                with sp.Fori(0, KF) as f:
                    for m in range(2):
                        sp.wait_ge(w_split, 2 * f + m + 1)
                        sp.dma_start(wt[:].rearrange("p (k f) -> p k f", k=KD), w_v[m][:, :, bass.ds(f * P, P)]).then_inc(w_loaded, 16)

            @block.gpsimd
            def _(pool):
                nc.gpsimd.memset(zero[:], 0.0)
                nc.gpsimd.drain().then_inc(w_split, 1)
                with pool.Fori(0, KF) as f:
                    for m in range(2):
                        hi, rest = w_hi[:, m].rearrange("p k f -> p (k f)"), w_lo[:, m].rearrange("p k f -> p (k f)")
                        pool.wait_ge(w_used, 2 * f + m + 1)
                        pool.wait_ge(w_loaded, 32 * f + 16 * m + 16)
                        nc.gpsimd.tensor_tensor(hi, wt[:], zero[:].to_broadcast([P, D]), ALU.subtract)
                        nc.gpsimd.drain()
                        nc.gpsimd.tensor_tensor(rest, wt[:], hi.bitcast(F32), ALU.subtract)
                        nc.gpsimd.drain().then_inc(w_split, 1)

            @block.tensor
            def _(pe):
                pe.sem_inc(w_used, 2)
                with pe.Fori(0, KF) as f:
                    for m in range(2):
                        pe.wait_ge(w_split, 2 * f + m + 2)
                        for g in range(G):
                            if m == 0:
                                pe.wait_ge(used, f * G + g + 1)
                            cols = slice(g * N, (g + 1) * N)
                            for k in range(KD):
                                for n, (w, x) in enumerate(((w_hi, xT), (w_hi, lo), (w_lo, xT))):
                                    last = nc.tensor.matmul(ps[:, g, m, 0:N], w[:, m, k, :], x[:, k, cols],
                                                            start=(k == 0 and n == 0), stop=(k == KD - 1 and n == 2))
                            last.then_inc((gate_done, up_done)[m], 1)
                        nc.tensor.drain().then_inc(w_used, 1)

            @block.scalar
            def _(act):
                with act.Fori(0, KF // WS) as i:
                    for s in range(WS):
                        for g in range(G):
                            u = (i * WS + s) * G + g
                            act.wait_ge(gate_done, u + 1)
                            act.wait_ge(gated, u + 1)
                            nc.scalar.activation(e[:, (s * G + g) % 2], ps[:, g, 0, 0:N], ACT.Tanh, scale=0.5).then_inc(e_ready, 1)

            @block.vector
            def _(dve):
                dve.sem_inc(used, G)
                dve.sem_inc(gated, 2)
                nc.vector.memset(hT[:, :, TOK:ROWS], 0.0)
                with dve.Fori(0, KF // WS) as i:
                    for s in range(WS):
                        out = lambda g: hT[:, bass.ds(i * WS + s, 1), g * N:(g + 1) * N].rearrange("p a n -> p (a n)")
                        for g in range(G):
                            dve.wait_ge(e_ready, (i * WS + s) * G + g + 1)
                            nc.vector.scalar_tensor_tensor(out=out(g), in0=e[:, (s * G + g) % 2], scalar=1.0, in1=ps[:, g, 0, 0:N],
                                                           op0=ALU.add, op1=ALU.mult)
                            nc.vector.drain().then_inc(gated, 1)
                        for g in range(G):
                            dve.wait_ge(up_done, (i * WS + s) * G + g + 1)
                            nc.vector.scalar_tensor_tensor(out=out(g), in0=out(g), scalar=0.5, in1=ps[:, g, 1, 0:N], op0=ALU.mult, op1=ALU.mult)
                            nc.vector.drain().then_inc(used, 1)


def final_norm(nc, tag, h, gain_row, y_prompt, y_sample):
    SLOTS = 3
    with ExitStack() as ctx:
        sb = lambda n, s: ctx.enter_context(nc.sbuf_tensor(f"{tag}_{n}", s, F32))
        sem = Sems(nc, ctx, tag)
        rows, sq, y = sb("rows", [P, SLOTS, D]), sb("sq", [P, D]), sb("y", [P, SLOTS, D])
        ss, sd, rs, eps = sb("ss", [P, SLOTS]), sb("sd", [P, SLOTS]), sb("rs", [P, SLOTS]), sb("eps", [P, 1])
        row_loaded, stored = sem("row_loaded", SLOTS), sem("stored", SLOTS)
        eps_set, row_free, sd_ready, normed = sem("eps_set"), sem("row_free"), sem("sd_ready"), sem("normed")
        with nc.Block() as block:

            @block.scalar
            def _(act):
                act.wait_ge(eps_set, 1)
                with act.Fori(0, TILES // SLOTS) as i:
                    for j in range(SLOTS):
                        act.wait_ge(row_free, i * SLOTS + j + 1)
                        act.dma_start(rows[:, j, :], h[bass.ds((i * SLOTS + j) * P, P), :]).then_inc(row_loaded[j], 16)
                    for j in range(SLOTS):
                        act.wait_ge(row_loaded[j], 16 * i + 16)
                        nc.scalar.activation(sq[:], rows[:, j, :], ACT.Square, accum_out=ss[:, j:j + 1])
                        nc.scalar.drain()
                        nc.scalar.activation(sd[:, j:j + 1], ss[:, j:j + 1], ACT.Sqrt, scale=1.0 / D,
                                             bias=eps[:, 0:1]).then_inc(sd_ready, 1)

            @block.vector
            def _(dve):
                nc.vector.memset(eps[:], EPS).then_inc(eps_set, 1)
                dve.sem_inc(row_free, SLOTS)
                with dve.Fori(0, TILES // SLOTS) as i:
                    for j in range(SLOTS):
                        dve.wait_ge(sd_ready, i * SLOTS + j + 1)
                        nc.vector.reciprocal(rs[:, j:j + 1], sd[:, j:j + 1])
                        nc.vector.drain()
                        dve.wait_ge(stored[j], 16 * i + 16)
                        nc.vector.scalar_tensor_tensor(out=y[:, j, :], in0=rows[:, j, :], scalar=rs[:, j:j + 1],
                                                       in1=gain_row, op0=ALU.mult, op1=ALU.mult).then_inc(normed, 1)
                        nc.vector.drain().then_inc(row_free, 1)

            @block.sync
            def _(sp):
                for j in range(SLOTS):
                    sp.sem_inc(stored[j], 16)
                with sp.Fori(0, TILES // SLOTS - 1) as i:
                    for j in range(SLOTS):
                        sp.wait_ge(normed, i * SLOTS + j + 1)
                        sp.dma_start(y_prompt[bass.ds((i * SLOTS + j) * P, P), :], y[:, j, :]).then_inc(stored[j], 16)
                for j in range(SLOTS):
                    t = TILES - SLOTS + j
                    sp.wait_ge(normed, t + 1)
                    if t < PT:
                        sp.dma_start(y_prompt[t * P:(t + 1) * P, :], y[:, j, :]).then_inc(stored[j], 16)
                    else:
                        sp.dma_start(y_sample, y[0:NS, j, :]).then_inc(stored[j], 16)
                for j in range(SLOTS):
                    sp.wait_ge(stored[j], 16 * (TILES // SLOTS) + 16)


def rope(nc, tag, z, segs, cos, sin, out):
    heads = sum(n for _, n in segs)
    HALF = DA // 2
    SLOTS = 3
    with ExitStack() as ctx:
        sb = lambda n, s: ctx.enter_context(nc.sbuf_tensor(f"{tag}_{n}", s, F32))
        sem = Sems(nc, ctx, tag)
        x, o = sb("x", [P, SLOTS, heads, 2, HALF]), sb("o", [P, SLOTS, heads, 2, HALF])
        cs = sb("cs", [P, SLOTS, 2, HALF])
        u1, u2 = sb("u1", [P, heads, HALF]), sb("u2", [P, heads, HALF])
        loaded, stored = sem("loaded", SLOTS), sem("stored", SLOTS)
        lo_done, hi_done = sem("lo_done"), sem("hi_done")
        with nc.Block() as block:

            @block.scalar
            def _(act):
                with act.Fori(0, TILES // SLOTS) as i:
                    for j in range(SLOTS):
                        t = i * SLOTS + j
                        row = bass.ds(t * P, P)
                        act.wait_ge(lo_done, t + 1)
                        act.wait_ge(hi_done, t + 1)
                        at = 0
                        for col, n in segs:
                            act.dma_start(x[:, j, at:at + n].rearrange("p h a d -> p (h a d)"), z[row, col:col + n * DA]).then_inc(loaded[j], 16)
                            at += n
                        act.dma_start(cs[:, j, 0], cos[row]).then_inc(loaded[j], 16)
                        act.dma_start(cs[:, j, 1], sin[row]).then_inc(loaded[j], 16)

            def rotate(eng, e, i, j, half, op, done):
                u = (u1, u2)[half]
                spread = lambda k: cs[:, j, k].unsqueeze(1).to_broadcast([P, heads, HALF])
                eng.wait_ge(loaded[j], 16 * (len(segs) + 2) * (i + 1))
                eng.wait_ge(stored[j], 16 * i + 16)
                e.tensor_tensor(o[:, j, :, half], x[:, j, :, half], spread(0), ALU.mult)
                e.tensor_tensor(u[:], x[:, j, :, 1 - half], spread(1), ALU.mult)
                e.drain()
                e.tensor_tensor(o[:, j, :, half], o[:, j, :, half], u[:], op)
                e.drain().then_inc(done, 1)

            @block.vector
            def _(dve):
                dve.sem_inc(lo_done, SLOTS)
                with dve.Fori(0, TILES // SLOTS) as i:
                    for j in range(SLOTS):
                        rotate(dve, nc.vector, i, j, 0, ALU.subtract, lo_done)

            @block.gpsimd
            def _(pool):
                pool.sem_inc(hi_done, SLOTS)
                with pool.Fori(0, TILES // SLOTS) as i:
                    for j in range(SLOTS):
                        rotate(pool, nc.gpsimd, i, j, 1, ALU.add, hi_done)

            @block.sync
            def _(sp):
                for j in range(SLOTS):
                    sp.sem_inc(stored[j], 16)
                with sp.Fori(0, TILES // SLOTS) as i:
                    for j in range(SLOTS):
                        t = i * SLOTS + j
                        sp.wait_ge(lo_done, t + 1 + SLOTS)
                        sp.wait_ge(hi_done, t + 1 + SLOTS)
                        sp.dma_start(out[bass.ds(t * P, P), :], o[:, j].rearrange("p h a d -> p (h a d)")).then_inc(stored[j], 16)
                for j in range(SLOTS):
                    sp.wait_ge(stored[j], 16 * (TILES // SLOTS) + 16)


def copy_rows(nc, tag, copies, also=(), also_done=None):
    with ExitStack() as ctx:
        sem = Sems(nc, ctx, tag)
        by_sync, by_act = sem("by_sync"), sem("by_act")
        with nc.Block() as block:

            @block.sync
            def _(sp):
                for dst, src in copies[0::2]:
                    sp.dma_start(dst, src).then_inc(by_sync, 16)
                for dst, src in also[0::2]:
                    sp.dma_start(dst, src).then_inc(also_done, 16)
                sp.wait_ge(by_sync, 16 * len(copies[0::2]))

            @block.scalar
            def _(act):
                for dst, src in copies[1::2]:
                    act.dma_start(dst, src).then_inc(by_act, 16)
                for dst, src in also[1::2]:
                    act.dma_start(dst, src).then_inc(also_done, 16)
                act.wait_ge(by_act, 16 * len(copies[1::2]))


def overlapped(eng, total, front, back):
    front(0, 0)
    with eng.Fori(0, total // 2 - 1) as i:
        front(2 * i + 1, 1)
        back(2 * i, 0)
        front(2 * i + 2, 0)
        back(2 * i + 1, 1)
    front(total - 1, 1)
    back(total - 2, 0)
    back(total - 1, 1)


def dilated_prompt(nc, tag, q, kv, mask, ident, out):
    TF = GA * PT
    SC = DA ** -0.5
    with ExitStack() as ctx:
        sb = lambda n, s: ctx.enter_context(nc.sbuf_tensor(f"{tag}_{n}", s, F32))
        pb = lambda n, s: ctx.enter_context(nc.psum_tensor(f"{tag}_{n}", s, F32))
        sem = Sems(nc, ctx, tag)
        qt, kvt, mt = sb("q", [P, 2, AW]), sb("kv", [P, 2, 2, 2 * AW]), sb("mask", [P, 2, 2 * P])
        qkT = sb("qkT", [P, 2, 3, P])
        s = sb("s", [P, 2, HA, 2 * P])
        mx, nm = sb("mx", [P, 2, HA]), sb("nm", [P, 2, HA])
        l, rl = sb("l", [P, 2, HA]), sb("rl", [P, 2, HA])
        ll = sb("ll", [P, 2, HA])
        pT = sb("pT", [P, HA, 2, P])
        ot = sb("ot", [P, 2, HA, DA + 1])
        psT, psS = pb("psT", [P, 2, 4, P]), pb("psS", [P, 2, 2, 2 * P])
        psP, psO = pb("psP", [P, HA, 2, P]), pb("psO", [P, HA, DA])
        loaded, stored, ot_free = sem("loaded", 2), sem("stored"), sem("ot_free")
        qk_turned, qk_copied, scored, masked = sem("qk_turned"), sem("qk_copied"), sem("scored"), sem("masked")
        max_ready, p_ready, p_turned, p_copied = sem("max_ready"), sem("p_ready"), sem("p_turned"), sem("p_copied", 2)
        o_done, tile_done = sem("o_done"), sem("tile_done")
        with nc.Block() as block:

            @block.sync
            def _(sp):
                with sp.Fori(0, TF // 2) as i:
                    for j in range(2):
                        f = 2 * i + j
                        sp.wait_ge(tile_done, f + 1)
                        sp.dma_start(qt[:, j], q[bass.ds(f * P, P), :]).then_inc(loaded[j], 16)
                        sp.dma_start(kvt[:, j], kv[bass.ds(f * P, 2 * P), :].rearrange("(a p) c -> p a c", p=P)).then_inc(loaded[j], 16)
                        sp.dma_start(mt[:, j], mask[bass.ds(f * P, P), :]).then_inc(loaded[j], 16)

            @block.tensor
            def _(pe):
                pe.sem_inc(p_turned, 2)
                pe.sem_inc(scored, 1)
                pe.sem_inc(o_done, 1)

                def front(f, j):
                    pe.wait_ge(loaded[j], 48 * ((f - j) // 2 + 1) if isinstance(f, int) else 24 * (f - j) + 48)
                    pe.wait_ge(qk_copied, f + 1)
                    for pair in range(2):
                        c = slice(pair * P, pair * P + P)
                        nc.tensor.transpose(psT[:, pair, 0], qt[:, j, c], ident)
                        nc.tensor.transpose(psT[:, pair, 1], kvt[:, j, 0, c], ident)
                        last = nc.tensor.transpose(psT[:, pair, 2], kvt[:, j, 1, c], ident)
                    last.then_inc(qk_turned, 1)
                    pe.wait_ge(qk_copied, f + 2)
                    pe.wait_ge(masked, f + 1)
                    for h in range(HA):
                        r = slice(DA * (h % 2), DA * (h % 2) + DA)
                        last = nc.tensor.matmul(psS[:, h % 2, h // 2], qkT[r, h // 2, 0], qkT[r, h // 2, 1:3], start=True, stop=True)
                        if h == HA - 1:
                            last.then_inc(scored, 1)

                def back(f, j):
                    pe.wait_ge(p_ready, f + 1)
                    pe.wait_ge(p_copied[0], f + 1)
                    pe.wait_ge(p_copied[1], f + 1)
                    for h in range(HA):
                        for a in range(2):
                            last = nc.tensor.transpose(psP[:, h, a], s[:, j, h, a * P:(a + 1) * P], ident)
                    last.then_inc(p_turned, 1)
                    pe.wait_ge(p_copied[0], f + 2)
                    pe.wait_ge(p_copied[1], f + 2)
                    pe.wait_ge(tile_done, f + 2)
                    for h in range(HA):
                        for a in range(2):
                            last = nc.tensor.matmul(psO[:, h], pT[:, h, a], kvt[:, j, a, AW + h * DA:AW + (h + 1) * DA],
                                                    start=(a == 0), stop=(a == 1))
                    last.then_inc(o_done, 1)

                overlapped(pe, TF, front, back)

            @block.scalar
            def _(act):
                act.sem_inc(qk_copied, 1)
                act.sem_inc(p_copied[1], 1)

                def front(f, j):
                    act.wait_ge(qk_turned, f + 1)
                    act.wait_ge(scored, f + 1)
                    nc.scalar.activation(qkT[:], psT[:, :, 0:3], ACT.Copy).then_inc(qk_copied, 1)

                def back(f, j):
                    act.wait_ge(max_ready, f + 1)
                    for h in range(HA):
                        nc.scalar.activation(s[:, j, h], s[:, j, h], ACT.Exp, scale=SC, bias=nm[:, j, h:h + 1],
                                             accum_out=l[:, j, h:h + 1])
                    nc.scalar.drain().then_inc(p_ready, 1)
                    nc.scalar.activation(ll[:, j], l[:, j], ACT.Ln)
                    act.wait_ge(p_turned, f + 3)
                    act.wait_ge(o_done, f + 1)
                    nc.scalar.activation(pT[:, 2:4], psP[:, 2:4], ACT.Copy)
                    nc.scalar.drain().then_inc(p_copied[1], 1)

                overlapped(act, TF, front, back)

            @block.vector
            def _(dve):
                dve.sem_inc(tile_done, 2)
                dve.sem_inc(masked, 1)
                dve.sem_inc(p_copied[0], 1)

                def front(f, j):
                    dve.wait_ge(scored, f + 2)
                    dve.wait_ge(loaded[j], 48 * ((f - j) // 2 + 1) if isinstance(f, int) else 24 * (f - j) + 48)
                    dve.wait_ge(p_turned, f + 1)
                    for b in range(2):
                        nc.vector.tensor_tensor(s[:, j, b::2], psS[:, b], mt[:, j].unsqueeze(1).to_broadcast([P, 2, 2 * P]), ALU.add)
                    nc.vector.drain().then_inc(masked, 1)
                    nc.vector.reduce_max(mx[:, j], s[:, j], AX.X)
                    nc.vector.drain()
                    nc.vector.tensor_scalar_mul(nm[:, j], mx[:, j], -SC).then_inc(max_ready, 1)

                def back(f, j):
                    dve.wait_ge(p_turned, f + 3)
                    dve.wait_ge(o_done, f + 1)
                    nc.vector.tensor_copy(pT[:, 0:2], psP[:, 0:2]).then_inc(p_copied[0], 1)
                    nc.vector.reciprocal(rl[:, j], l[:, j])
                    nc.vector.drain()
                    dve.wait_ge(ot_free, f + 1)
                    dve.wait_ge(p_copied[1], f + 2)
                    nc.vector.tensor_tensor(ot[:, j, :, DA], ll[:, j], nm[:, j], ALU.subtract)
                    dve.wait_ge(o_done, f + 2)
                    nc.vector.tensor_tensor(ot[:, j, :, 0:DA], psO[:],
                                            rl[:, j].unsqueeze(2).to_broadcast([P, HA, DA]), ALU.mult)
                    nc.vector.drain().then_inc(tile_done, 1)

                overlapped(dve, TF, front, back)

            @block.gpsimd
            def _(pool):
                pool.sem_inc(ot_free, 2)
                with pool.Fori(0, TF // 2) as i:
                    for j in range(2):
                        pool.wait_ge(tile_done, 2 * i + j + 3)
                        pool.dma_start(out[bass.ds((2 * i + j) * P, P), :], ot[:, j].rearrange("p h d -> p (h d)")).then_inc(stored, 16)
                        pool.wait_ge(stored, 32 * i + 16 * j + 16)
                        pool.sem_inc(ot_free, 1)


def mlstm_gates(nc, tag, z, b_if, m0, ident, Mrow, cols, dec, dec_s, dec_sT, bm_p, bm_s):
    S0 = SEQ
    with ExitStack() as ctx:
        sb = lambda n, s: ctx.enter_context(nc.sbuf_tensor(f"{tag}_{n}", s, F32))
        pb = lambda n, s: ctx.enter_context(nc.psum_tensor(f"{tag}_{n}", s, F32))
        sem = Sems(nc, ctx, tag)
        zg = sb("zg", [P, TILES, 2 * HB])
        bias = sb("bias", [HB, 2])
        ig, x, t1, t2 = (sb(n, [HB, TOK]) for n in ("ig", "x", "t1", "t2"))
        b, one = sb("b", [HB, TOK]), sb("one", [HB, P])
        kinds = sb("kinds", [HB, 4, TOK])
        mstart = sb("mstart", [HB, PT + 1])
        nMl, nMs = sb("nMl", [HB, PT]), sb("nMs", [HB, DEC_B])
        m0t, mS, d0 = sb("m0t", [HB, DEC_B]), sb("mS", [HB, DEC_B]), sb("d0", [HB, DEC_B])
        dg = sb("dg", [HB, PT, HB])
        dgs = sb("dgs", [HB, HB, DEC_B])
        ones = sb("ones", [HB, P])
        psG = pb("psG", [HB, 5, 512])
        psC = pb("psC", [P, TILES, 4, HB])
        psD = pb("psD", [P, 128])
        loaded, stored = sem("loaded"), sem("stored")
        turned, biased, lns, lfs, stab, expd, c_turned, diag, spread = (
            sem(n) for n in ("turned", "biased", "lns", "lfs", "stab", "expd", "c_turned", "diag", "spread"))
        gT = psG[:].rearrange("h a b -> h (a b)")
        cs = lambda c: slice(c * P, c * P + P)
        sam = lambda ap: ap[:, S0:TOK].rearrange("h (b t) -> h b t", t=DEC_T)
        with nc.Block() as block:

            @block.sync
            def _(sp):
                sp.dma_start(zg[:], z[:, OFF_IG:OFF_IG + 2 * HB].rearrange("(t p) c -> p t c", p=P)).then_inc(loaded, 16)
                sp.dma_start(bias[:], b_if.rearrange("a h -> h a"), allow_slow_non_contiguous=True).then_inc(loaded, 16)
                sp.dma_start(m0t[:], m0.rearrange("b h -> h b"), allow_slow_non_contiguous=True).then_inc(loaded, 16)
                sp.wait_ge(stab, 1)
                sp.dma_start(bm_p.rearrange("b h -> h b"), mstart[:, PT:PT + 1], allow_slow_non_contiguous=True).then_inc(stored, 16)
                sp.dma_start(bm_s.rearrange("b h -> h b"), mS[:], allow_slow_non_contiguous=True).then_inc(stored, 16)
                sp.wait_ge(stored, 32)

            @block.tensor
            def _(pe):
                pe.wait_ge(loaded, 48)
                for a in range(2):
                    for t in range(TILES):
                        last = nc.tensor.transpose(gT[:, a * ROWS + t * P:a * ROWS + t * P + P], zg[:, t, a * HB:a * HB + HB], ident)
                last.then_inc(turned, 1)
                pe.wait_ge(expd, 1)
                for t in range(TILES):
                    n = min(P, TOK - t * P)
                    for k in range(4):
                        last = nc.tensor.transpose(psC[0:n, t, k], kinds[:, k, t * P:t * P + n], ident[0:HB, 0:HB])
                last.then_inc(c_turned, 1)
                pe.wait_ge(diag, 1)
                nc.tensor.matmul(psD[:, 0:PT * HB], ones[:], dg[:].rearrange("h c k -> h (c k)"), start=True, stop=True)
                nc.tensor.matmul(psD[:, 32:64], ones[:], dgs[:].rearrange("h k b -> h (k b)"), start=True, stop=True)
                nc.tensor.transpose(psD[0:DEC_B, 64:64 + HB], d0[:], ident[0:HB, 0:HB]).then_inc(spread, 1)

            @block.vector
            def _(dve):
                v = nc.vector
                v.memset(one[:], 1.0)
                v.memset(ones[:], 1.0)
                dve.wait_ge(turned, 1)
                v.tensor_scalar(ig[:], gT[:, 0:TOK], bias[:, 0:1], None, ALU.add)
                v.tensor_scalar(x[:], gT[:, ROWS:ROWS + TOK], bias[:, 1:2], None, ALU.add)
                v.drain()
                v.drain()
                v.scalar_tensor_tensor(out=t1[:], in0=x[:], scalar=-1.0, in1=x[:], op0=ALU.mult, op1=ALU.min)
                v.drain()
                v.tensor_scalar_min(x[:], x[:], 0.0)
                v.drain().then_inc(biased, 1)
                dve.wait_ge(lns, 1)
                v.tensor_tensor(x[:], x[:], t2[:], ALU.subtract)
                v.memset(mstart[:, 0:1], 0.0)
                v.drain()
                c = kinds[:, 0]
                for k in range(PT):
                    v.tensor_tensor_scan(b[:, cs(k)], one[:], x[:, cs(k)], 0.0, ALU.mult, ALU.add)
                bs, xs = sam(b), sam(x)
                v.tensor_copy(bs[:, :, 0], xs[:, :, 0])
                for t in range(1, DEC_T):
                    v.drain()
                    v.tensor_tensor(bs[:, :, t], bs[:, :, t - 1], xs[:, :, t], ALU.add)
                v.drain()
                v.tensor_tensor(c, ig[:], b[:], ALU.subtract)
                v.drain()
                for k in range(PT):
                    v.tensor_tensor_scan(Mrow[:, cs(k)], c[:, cs(k)], c[:, cs(k)], mstart[:, k:k + 1], ALU.max, ALU.max)
                    v.drain()
                    last = slice(k * P + P - 1, k * P + P)
                    v.tensor_tensor(mstart[:, k + 1:k + 2], b[:, last], Mrow[:, last], ALU.add)
                    v.tensor_scalar_mul(nMl[:, k:k + 1], Mrow[:, last], -1.0)
                    v.drain()
                Ms, c_s = sam(Mrow), sam(c)
                v.tensor_tensor(Ms[:, :, 0], m0t[:], c_s[:, :, 0], ALU.max)
                for t in range(1, DEC_T):
                    v.drain()
                    v.tensor_tensor(Ms[:, :, t], Ms[:, :, t - 1], c_s[:, :, t], ALU.max)
                v.drain()
                v.tensor_tensor(mS[:], bs[:, :, DEC_T - 1], Ms[:, :, DEC_T - 1], ALU.add)
                v.tensor_tensor(sam(kinds[:, 1]), c_s, Ms[:, :, DEC_T - 1:DEC_T].to_broadcast([HB, DEC_B, DEC_T]), ALU.subtract)
                v.tensor_tensor(sam(kinds[:, 2]), m0t[:].unsqueeze(2).to_broadcast([HB, DEC_B, DEC_T]), Ms, ALU.subtract)
                v.tensor_tensor(kinds[:, 3], b[:], Mrow[:, 0:TOK], ALU.add)
                v.drain().then_inc(stab, 1)
                dve.wait_ge(expd, 1)
                for k in range(PT):
                    v.tensor_scalar(dg[:, k], ident[0:HB, 0:HB], kinds[:, 2, k * P + P - 1:k * P + P], None, ALU.mult)
                v.tensor_copy(d0[:], sam(kinds[:, 2])[:, :, DEC_T - 1])
                v.tensor_tensor(dgs[:], ident[0:HB, 0:HB].unsqueeze(2).to_broadcast([HB, HB, DEC_B]),
                                sam(kinds[:, 2])[:, :, DEC_T - 1].unsqueeze(1).to_broadcast([HB, HB, DEC_B]), ALU.mult)
                v.drain().then_inc(diag, 1)
                dve.wait_ge(c_turned, 1)
                v.tensor_copy(cols[:, 0:PT], psC[:, 0:PT])
                v.tensor_copy(cols[0:NS, PT], psC[0:NS, PT])
                dve.wait_ge(spread, 1)
                v.tensor_copy(dec, psD[:, 0:PT * HB].rearrange("p (c h) -> p c h", h=HB))
                v.tensor_copy(dec_s, psD[:, 32:64].rearrange("p (h b) -> p h b", h=HB))
                v.tensor_copy(dec_sT, psD[0:DEC_B, 64:64 + HB])

            @block.scalar
            def _(act):
                a = nc.scalar
                act.wait_ge(biased, 1)
                a.activation(t2[:], t1[:], ACT.Exp)
                a.drain()
                a.activation(t2[:], t2[:], ACT.Ln, bias=1.0).then_inc(lns, 1)
                act.wait_ge(stab, 1)
                for k in range(PT):
                    a.activation(kinds[:, 1, cs(k)], kinds[:, 0, cs(k)], ACT.Exp, bias=nMl[:, k:k + 1])
                    a.activation(kinds[:, 2, cs(k)], Mrow[:, cs(k)], ACT.Exp, scale=-1.0, bias=mstart[:, k:k + 1])
                a.activation(kinds[:, 1:3, S0:TOK], kinds[:, 1:3, S0:TOK], ACT.Exp)
                a.activation(kinds[:, 3], kinds[:, 3], ACT.Exp, scale=-1.0)
                a.drain().then_inc(expd, 1)


def mlstm_prompt(nc, tag, z, Mrow, cols, dec, rowsel, later, ident, h_out, C_out, n_out):
    V1 = DB + 1
    with ExitStack() as ctx:
        sb = lambda n, s: ctx.enter_context(nc.sbuf_tensor(f"{tag}_{n}", s, F32))
        pb = lambda n, s: ctx.enter_context(nc.psum_tensor(f"{tag}_{n}", s, F32))
        sem = Sems(nc, ctx, tag)
        qk = sb("qk", [P, 2, 2, HB, DB])
        va = sb("va", [P, 2, HB, V1])
        qkT = sb("qkT", [P, 2, HB, P])
        mrow = sb("mrow", [HB, 2, P])
        dw, sc = sb("dw", [P, HB, P]), sb("sc", [P, HB, P])
        wv, C = sb("wv", [P, HB, V1]), sb("C", [P, HB, V1])
        inter, tot = sb("inter", [P, HB, V1]), sb("tot", [P, HB, V1])
        r, hb = sb("r", [P, HB]), sb("hb", [P, 2, HB, DB])
        CT = sb("CT", [P, HB, DB])
        ccol, iwcol, wlcol, emcol, dcol = (sb(n, [P, HB]) for n in ("ccol", "iwcol", "wlcol", "emcol", "dcol"))
        psT = pb("psT", [P, 2, 512])
        psM = pb("psM", [P, HB, P])
        psS = pb("psS", [P, HB, P])
        psN = pb("psN", [P, 2, 512])
        psI = pb("psI", [P, 2, 512])
        loaded, stored, hb_free = sem("loaded", 2), sem("stored"), sem("hb_free")
        prepared, turned, m_spread, qkT_ready, scored, dw_ready, sc_ready, sum_done, inter_read, upd_done, chunk_done, final = (
            sem(n) for n in ("prepared", "turned", "m_spread", "qkT_ready", "scored", "dw_ready", "sc_ready", "sum_done",
                             "inter_read", "upd_done", "chunk_done", "final"))
        args_ready, state_stored = sem("args_ready"), sem("state_stored")
        two = lambda ps, h: ps[:, h // 2, (h % 2) * V1:(h % 2) * V1 + V1]
        all4 = lambda ps: ps[:, :, 0:2 * V1].rearrange("p a (b e) -> p a b e", b=2)
        with nc.Block() as block:

            @block.sync
            def _(sp):
                with sp.Fori(0, PT // 2) as i:
                    for j in range(2):
                        sp.wait_ge(chunk_done, 2 * i + j + 1)
                        row = bass.ds((2 * i + j) * P, P)
                        sp.dma_start(qk[:, j].rearrange("p a h d -> p (a h d)"), z[row, OFF_QB:OFF_QB + 2 * BW]).then_inc(loaded[j], 16)
                        sp.dma_start(va[:, j, :, 0:DB], z[row, OFF_VB:OFF_VB + BW].rearrange("p (h d) -> p h d", h=HB)).then_inc(loaded[j], 16)
                sp.wait_ge(hb_free, PT + 2)
                sp.wait_ge(final, 1)
                sp.dma_start(C_out.rearrange("h e d -> e h d"), CT[:]).then_inc(state_stored, 16)
                sp.dma_start(n_out.rearrange("h (d o) -> d h o", o=1), C[:, :, DB:V1], allow_slow_non_contiguous=True).then_inc(state_stored, 16)
                sp.wait_ge(state_stored, 32)

            @block.tensor
            def _(pe):
                with pe.Fori(0, PT // 2) as i:
                    for j in range(2):
                        c = 2 * i + j
                        pe.wait_ge(prepared, c + 1)
                        for a in range(2):
                            for h in range(HB):
                                last = nc.tensor.transpose(psT[:, a, h * P:h * P + P], qk[:, j, a, h], ident)
                        last.then_inc(turned, 1)
                        for h in range(HB):
                            last = nc.tensor.matmul(psM[:, h], rowsel[:, h], mrow[:, j], start=True, stop=True)
                        last.then_inc(m_spread, 1)
                        pe.wait_ge(qkT_ready, c + 1)
                        for h in range(HB):
                            nc.tensor.matmul(psS[:, h], qkT[:, 1, h], qkT[:, 0, h], start=True, stop=True)
                        for h in range(HB):
                            last = nc.tensor.matmul(two(psI, h), qkT[:, 0, h], C[:, h], start=True, stop=True)
                        last.then_inc(scored, 1)
                        pe.wait_ge(sc_ready, c + 1)
                        for h in range(HB):
                            last = nc.tensor.matmul(two(psN, h), sc[:, h], va[:, j, h], start=True, stop=True)
                        last.then_inc(sum_done, 1)
                        pe.wait_ge(inter_read, c + 1)
                        for h in range(HB):
                            last = nc.tensor.matmul(two(psI, h), qk[:, j, 1, h], wv[:, h], start=True, stop=True)
                        last.then_inc(upd_done, 1)
                pe.wait_ge(chunk_done, PT + 2)
                for h in range(HB):
                    last = nc.tensor.transpose(psT[:, 0, h * P:h * P + P], C[:, h, 0:DB], ident)
                last.then_inc(turned, 1)

            @block.scalar
            def _(act):
                a = nc.scalar
                with act.Fori(0, PT // 2) as i:
                    for j in range(2):
                        c = 2 * i + j
                        act.wait_ge(turned, c + 1)
                        a.activation(qkT[:].rearrange("p a h t -> p a (h t)"), psT[:], ACT.Copy).then_inc(qkT_ready, 1)
                        act.wait_ge(args_ready, c + 1)
                        a.activation(dw[:], dw[:], ACT.Exp, scale=-1.0).then_inc(dw_ready, 1)
                        act.wait_ge(scored, c + 1)
                        act.wait_ge(chunk_done, c + 2)
                        for h in range(HB):
                            a.activation(inter[:, h], two(psI, h), ACT.Copy, scale=iwcol[:, h:h + 1])
                        a.drain().then_inc(inter_read, 1)
                act.wait_ge(turned, PT + 1)
                a.activation(CT[:].rearrange("p h d -> p (h d)"), psT[:, 0], ACT.Copy).then_inc(final, 1)

            @block.vector
            def _(dve):
                v = nc.vector
                v.memset(C[:], 0.0)
                v.memset(va[:, :, :, DB:V1], 1.0)
                dve.sem_inc(chunk_done, 2)
                with dve.Fori(0, PT // 2) as i:
                    for j in range(2):
                        c = 2 * i + j
                        one = bass.ds(c, 1)
                        v.tensor_copy(mrow[:, j], Mrow[:, bass.ds(c * P, P)])
                        for k, to in ((0, ccol), (1, wlcol), (2, iwcol), (3, emcol)):
                            v.tensor_copy(to[:], cols[:, one, k].rearrange("p a h -> p (a h)"))
                        v.tensor_copy(dcol[:], dec[:, one].rearrange("p a h -> p (a h)"))
                        dve.wait_ge(loaded[j], 32 * i + 32)
                        v.tensor_scalar_mul(qk[:, j, 1], qk[:, j, 1], DB ** -0.5)
                        v.drain().then_inc(prepared, 1)
                        for h in range(HB):
                            v.tensor_scalar(wv[:, h], va[:, j, h], wlcol[:, h:h + 1], None, ALU.mult)
                        dve.wait_ge(m_spread, c + 1)
                        for h in range(HB):
                            v.scalar_tensor_tensor(out=dw[:, h], in0=psM[:, h], scalar=ccol[:, h:h + 1], in1=later,
                                                   op0=ALU.subtract, op1=ALU.add)
                        v.drain().then_inc(args_ready, 1)
                        dve.wait_ge(dw_ready, c + 1)
                        dve.wait_ge(scored, c + 1)
                        v.tensor_tensor(sc[:], psS[:], dw[:], ALU.mult).then_inc(sc_ready, 1)
                        dve.wait_ge(sum_done, c + 1)
                        dve.wait_ge(inter_read, c + 1)
                        v.tensor_tensor(tot[:].rearrange("p (a b) e -> p a b e", b=2), all4(psN),
                                        inter[:].rearrange("p (a b) e -> p a b e", b=2), ALU.add)
                        v.drain()
                        v.scalar_tensor_tensor(out=r[:], in0=tot[:, :, DB], scalar=-1.0, in1=tot[:, :, DB], op0=ALU.mult, op1=ALU.max)
                        v.drain()
                        v.tensor_tensor(r[:], r[:], emcol[:], ALU.max)
                        v.drain()
                        v.reciprocal(r[:], r[:])
                        v.drain()
                        dve.wait_ge(hb_free, c + 1)
                        v.tensor_tensor(hb[:, j], tot[:, :, 0:DB], r[:].unsqueeze(2).to_broadcast([P, HB, DB]), ALU.mult)
                        dve.wait_ge(upd_done, c + 1)
                        for h in range(HB):
                            v.scalar_tensor_tensor(out=C[:, h], in0=C[:, h], scalar=dcol[:, h:h + 1], in1=two(psI, h),
                                                   op0=ALU.mult, op1=ALU.add)
                        v.drain().then_inc(chunk_done, 1)

            @block.gpsimd
            def _(pool):
                pool.sem_inc(hb_free, 2)
                with pool.Fori(0, PT // 2) as i:
                    for j in range(2):
                        pool.wait_ge(chunk_done, 2 * i + j + 3)
                        pool.dma_start(h_out[bass.ds((2 * i + j) * P, P), :], hb[:, j].rearrange("p h d -> p (h d)")).then_inc(stored, 16)
                        pool.wait_ge(stored, 32 * i + 16 * j + 16)
                        pool.sem_inc(hb_free, 1)


def mlstm_sample(nc, tag, z, Mrow, cols, dec_s, dec_sT, rowsel, later_s, own, own_cols, C0, n0, ident, h_out, C_out, n_out):
    V1 = DB + 1
    with ExitStack() as ctx:
        sb = lambda n, s: ctx.enter_context(nc.sbuf_tensor(f"{tag}_{n}", s, F32))
        pb = lambda n, s: ctx.enter_context(nc.psum_tensor(f"{tag}_{n}", s, F32))
        sem = Sems(nc, ctx, tag)
        qk, va = sb("qk", [NS, 2, HB, DB]), sb("va", [NS, HB, V1])
        Ct = sb("C", [P, DEC_B, HB, DB])
        nt, nr = sb("nt", [DEC_B * HB, DB]), sb("nr", [DEC_B, HB, DB])
        CT = sb("CT", [P, 2, DEC_B, V1])
        qkT = sb("qkT", [P, 2, HB, NS])
        qm = sb("qm", [P, HB, DEC_B, NS])
        dw, sc = sb("dw", [NS, HB, NS]), sb("sc", [NS, HB, NS])
        wv = sb("wv", [NS, HB, V1])
        wvm = sb("wvm", [NS, HB, DEC_B, DB])
        wlm = sb("wlm", [NS, HB, DEC_B])
        inter, tot, r = sb("inter", [NS, HB, V1]), sb("tot", [NS, HB, V1]), sb("r", [NS, HB])
        hb = sb("hb", [NS, HB, DB])
        Cn, nn, nT = sb("Cn", [P, DEC_B, HB, DB]), sb("nn", [DEC_B, HB, DB]), sb("nT", [P, DEC_B * HB])
        psT = pb("psT", [P, 512])
        psS, psM = pb("psS", [NS, HB, NS]), pb("psM", [NS, HB, NS])
        psC = pb("psC", [P, 2, 4, DB])
        psI, psN = pb("psI", [NS, 512]), pb("psN", [NS, 2, 512])
        loaded, stored = sem("loaded"), sem("stored")
        scaled, turned, T_ready, made, scored, dw_ready, sc_ready, c_turned, c_copied, summed, summed_read, intra, upd, upd_read, n_upd = (
            sem(n) for n in ("scaled", "turned", "T_ready", "made", "scored", "dw_ready", "sc_ready", "c_turned", "c_copied",
                             "summed", "summed_read", "intra", "upd", "upd_read", "n_upd"))
        tot_done, h_done, n_done = sem("tot_done"), sem("h_done"), sem("n_done")
        row = slice(SEQ, TOK)
        two = lambda ps, h: ps[:, h // 2, (h % 2) * V1:(h % 2) * V1 + V1]
        all4 = lambda ps: ps[:, :, 0:2 * V1].rearrange("p a (b e) -> p a b e", b=2)
        with nc.Block() as block:

            @block.sync
            def _(sp):
                sp.dma_start(qk[:].rearrange("p a h d -> p (a h d)"), z[row, OFF_QB:OFF_QB + 2 * BW]).then_inc(loaded, 16)
                sp.dma_start(va[:, :, 0:DB], z[row, OFF_VB:OFF_VB + BW].rearrange("p (h d) -> p h d", h=HB)).then_inc(loaded, 16)
                sp.dma_start(nt[:], n0.rearrange("b h d -> (b h) d")).then_inc(loaded, 16)
                sp.dma_start(nr[:], n0).then_inc(loaded, 16)
                sp.dma_start(Ct[:].rearrange("e b h d -> e (b h) d"), C0.rearrange("b h e d -> e (b h) d")).then_inc(loaded, 16)
                sp.wait_ge(h_done, 1)
                sp.dma_start(h_out[row, :], hb[:].rearrange("p h d -> p (h d)")).then_inc(stored, 16)
                sp.wait_ge(upd_read, 2 * HB)
                sp.dma_start(C_out.rearrange("b h e d -> e (b h) d"), Cn[:].rearrange("e b h d -> e (b h) d")).then_inc(stored, 16)
                sp.wait_ge(n_done, 1)
                sp.dma_start(n_out, nn[:]).then_inc(stored, 16)
                sp.wait_ge(stored, 48)

            @block.tensor
            def _(pe):
                T, M = nc.tensor.transpose, nc.tensor.matmul
                pe.wait_ge(scaled, 1)
                for a in range(2):
                    for h in range(HB):
                        T(psT[:, (a * HB + h) * NS:(a * HB + h + 1) * NS], qk[:, a, h], ident[0:NS, 0:NS])
                T(psT[:, 2 * HB * NS:2 * HB * NS + NS], nt[:], ident[0:NS, 0:NS]).then_inc(turned, 1)
                for h in range(HB):
                    last = M(psM[:, h], rowsel[:, h, 0:NS], Mrow[:, row], start=True, stop=True)
                last.then_inc(turned, 1)
                pe.wait_ge(T_ready, 1)
                for h in range(HB):
                    last = M(psS[:, h], qkT[:, 1, h], qkT[:, 0, h], start=True, stop=True)
                last.then_inc(scored, 1)
                for h in range(HB):
                    if h:
                        pe.wait_ge(c_copied, 2 * h)
                    for b in range(DEC_B):
                        last = T(psC[:, b // 4, b % 4], Ct[:, b, h], ident)
                    last.then_inc(c_turned, 1)
                    pe.wait_ge(c_copied, 2 * h + 2)
                    pe.wait_ge(made, 1)
                    if h:
                        pe.wait_ge(summed_read, h)
                    for b in range(DEC_B):
                        last = M(psI[:, 0:V1], qm[:, h, b], CT[:, h % 2, b], start=(b == 0), stop=(b == DEC_B - 1))
                    last.then_inc(summed, 1)
                pe.wait_ge(sc_ready, 1)
                for h in range(HB):
                    last = M(two(psN, h), sc[:, h], va[:, h], start=True, stop=True)
                last.then_inc(intra, 1)
                for h in range(HB):
                    for a in range(2):
                        if h:
                            pe.wait_ge(upd_read, 2 * h - 1 + a)
                        for b in range(4):
                            last = M(psC[:, a, b], wvm[:, h, 4 * a + b], qk[:, 1, h], start=True, stop=True)
                        last.then_inc(upd, 1)
                pe.wait_ge(tot_done, 1)
                for h in range(HB):
                    last = M(psN[0:DEC_B, 0, h * DB:(h + 1) * DB], wlm[:, h], qk[:, 1, h], start=True, stop=True)
                last.then_inc(n_upd, 1)

            @block.scalar
            def _(act):
                a = nc.scalar
                act.wait_ge(turned, 1)
                a.activation(qkT[:].rearrange("p a h t -> p (a h t)"), psT[:, 0:2 * HB * NS], ACT.Copy)
                a.activation(nT[:], psT[:, 2 * HB * NS:2 * HB * NS + NS], ACT.Copy)
                a.drain().then_inc(T_ready, 1)
                act.wait_ge(made, 1)
                a.activation(dw[:], dw[:], ACT.Exp, scale=-1.0).then_inc(dw_ready, 1)
                for h in range(HB):
                    act.wait_ge(c_turned, h + 1)
                    if h > 1:
                        act.wait_ge(summed, h - 1)
                    for k in range(2):
                        a.activation(CT[:, h % 2, 4 * k:4 * k + 4, 0:DB], psC[:, k], ACT.Copy)
                    a.activation(CT[:, h % 2, :, DB], nT[:, h::HB], ACT.Copy)
                    a.drain().then_inc(c_copied, 2)
                    act.wait_ge(summed, h + 1)
                    a.activation(inter[:, h], psI[:, 0:V1], ACT.Copy, scale=cols[0:NS, PT, 2, h:h + 1])
                    a.drain().then_inc(summed_read, 1)

            @block.vector
            def _(dve):
                v = nc.vector
                v.memset(va[:, :, DB:V1], 1.0)
                dve.wait_ge(loaded, 80)
                v.tensor_scalar_mul(qk[:, 1], qk[:, 1], DB ** -0.5)
                v.drain().then_inc(scaled, 1)
                wl = cols[0:NS, PT, 1]
                v.tensor_tensor(wv[:], va[:], wl.unsqueeze(2).to_broadcast([NS, HB, V1]), ALU.mult)
                v.tensor_tensor(wlm[:], wl.unsqueeze(2).to_broadcast([NS, HB, DEC_B]), own.unsqueeze(1).to_broadcast([NS, HB, DEC_B]), ALU.mult)
                v.drain()
                for h in range(HB):
                    v.tensor_tensor(wvm[:, h], wv[:, h, 0:DB].unsqueeze(1).to_broadcast([NS, DEC_B, DB]),
                                    own.unsqueeze(2).to_broadcast([NS, DEC_B, DB]), ALU.mult)
                dve.wait_ge(turned, 2)
                for h in range(HB):
                    v.scalar_tensor_tensor(out=dw[:, h], in0=psM[:, h], scalar=cols[0:NS, PT, 0, h:h + 1], in1=later_s,
                                           op0=ALU.subtract, op1=ALU.add)
                dve.wait_ge(T_ready, 1)
                for h in range(HB):
                    v.tensor_tensor(qm[:, h], qkT[:, 0, h].unsqueeze(1).to_broadcast([P, DEC_B, NS]), own_cols, ALU.mult)
                v.drain().then_inc(made, 1)
                dve.wait_ge(dw_ready, 1)
                dve.wait_ge(scored, 1)
                v.tensor_tensor(sc[:], psS[:], dw[:], ALU.mult).then_inc(sc_ready, 1)
                dve.wait_ge(intra, 1)
                dve.wait_ge(summed_read, HB)
                v.tensor_tensor(tot[:].rearrange("p (a b) e -> p a b e", b=2), all4(psN), inter[:].rearrange("p (a b) e -> p a b e", b=2), ALU.add)
                v.drain().then_inc(tot_done, 1)
                v.scalar_tensor_tensor(out=r[:], in0=tot[:, :, DB], scalar=-1.0, in1=tot[:, :, DB], op0=ALU.mult, op1=ALU.max)
                v.drain()
                v.tensor_tensor(r[:], r[:], cols[0:NS, PT, 3], ALU.max)
                v.drain()
                v.reciprocal(r[:], r[:])
                v.drain()
                v.tensor_tensor(hb[:], tot[:, :, 0:DB], r[:].unsqueeze(2).to_broadcast([NS, HB, DB]), ALU.mult).then_inc(h_done, 1)
                for h in range(HB):
                    for k in range(2):
                        dve.wait_ge(upd, 2 * h + k + 1)
                        for b in range(4 * k, 4 * k + 4):
                            v.scalar_tensor_tensor(out=Cn[:, b, h], in0=Ct[:, b, h], scalar=dec_s[:, h, b:b + 1], in1=psC[:, k, b % 4],
                                                   op0=ALU.mult, op1=ALU.add)
                        v.drain().then_inc(upd_read, 1)
                v.tensor_tensor(nn[:], nr[:], dec_sT.unsqueeze(2).to_broadcast([DEC_B, HB, DB]), ALU.mult)
                v.drain()
                dve.wait_ge(n_upd, 1)
                v.tensor_tensor(nn[:], nn[:], psN[0:DEC_B, 0].rearrange("p (h d) -> p h d", h=HB), ALU.add).then_inc(n_done, 1)


def dilated_sample(nc, tag, qk, z, caches, masks, ident, outs):
    SC = DA ** -0.5
    RING = 4
    row = slice(SEQ, TOK)
    with ExitStack() as ctx:
        sb = lambda n, s: ctx.enter_context(nc.sbuf_tensor(f"{tag}_{n}", s, F32))
        pb = lambda n, s: ctx.enter_context(nc.psum_tensor(f"{tag}_{n}", s, F32))
        sem = Sems(nc, ctx, tag)
        kv = [sb(f"kv{g}", [P, DEC_B, 1 if g == 0 else DEC_T, 2 * AW]) for g in range(GA)]
        qb = sb("qb", [P, RING, DEC_T, AW])
        prod = sb("prod", [P, DEC_T * HA, DA])
        new = sb("new", [NS, 3, GA, AW])
        nT = sb("nT", [DA, 2, HA, NS])
        S = sb("S", [P, HA, DEC_B, DEC_T])
        s, mk = sb("s", [P, P + NS]), sb("mk", [P, GA, P + NS])
        mx, nm, l, rl, ll = (sb(n, [P, 1]) for n in ("mx", "nm", "l", "rl", "ll"))
        pT, pnT = sb("pT", [P, P]), sb("pnT", [NS, P])
        oT, o = sb("oT", [DA, P]), sb("o", [P, GA, DA + 1])
        psN, psT, psA, psB = pb("psN", [P, 512]), pb("psT", [P, 2, 4, P]), pb("psA", [P, 512]), pb("psB", [P, 512])
        psO, psO2, psR = pb("psO", [P, 512]), pb("psO2", [P, 512]), pb("psR", [P, 512])
        kv_loaded, q_loaded, new_loaded, mask_loaded = sem("kv_loaded", GA), sem("q_loaded", RING), sem("new_loaded"), sem("mask_loaded")
        q_used, dots_done, n_turned, n_copied, s_turned, s_ready, max_ready, p_ready = (
            sem(n) for n in ("q_used", "dots_done", "n_turned", "n_copied", "s_turned", "s_ready", "max_ready", "p_ready"))
        p_turned, p_copied, o_summed, oT_ready, o_turned, o_ready, stored = (
            sem(n) for n in ("p_turned", "p_copied", "o_summed", "oT_ready", "o_turned", "o_ready", "stored"))
        with nc.Block() as block:

            @block.sync
            def _(sp):
                for a, (src, col) in enumerate(((qk, 0), (qk, QA), (z, OFF_VA))):
                    sp.dma_start(new[:, a].rearrange("p g c -> p (g c)"), src[row, col:col + QA]).then_inc(new_loaded, 16)
                sp.dma_start(mk[:], masks).then_inc(mask_loaded, 16)
                for g, (win, dil) in enumerate(DIL):
                    n = 1 if g == 0 else DEC_T
                    for b in range(DEC_B):
                        sp.dma_start(kv[g][:, b], caches[g][b].rearrange("(j r) c -> j r c", r=dil)[:, 0:n, :]).then_inc(kv_loaded[g], 16)
                for g in range(GA):
                    sp.wait_ge(o_ready, g + 1)
                    for h in range(HA):
                        sp.dma_start(outs[g][row, h * (DA + 1):(h + 1) * (DA + 1)], o[NS * h:NS * h + NS, g]).then_inc(stored, 16)
                sp.wait_ge(stored, 16 * GA * HA)

            @block.gpsimd
            def _(pool):
                for g in range(GA):
                    with pool.Fori(0, DEC_B // RING) as i:
                        for r in range(RING):
                            b = i * RING + r
                            pool.wait_ge(q_used, g * DEC_B + b + 1)
                            pool.dma_start(qb[:, r], qk[bass.ds(SEQ + b * DEC_T, DEC_T), g * AW:(g + 1) * AW].unsqueeze(0)
                                           .to_broadcast([P, DEC_T, AW])).then_inc(q_loaded[r], 16)

            @block.scalar
            def _(act):
                a = nc.scalar
                for g in range(GA):
                    act.wait_ge(n_turned, g + 1)
                    a.activation(nT[:].rearrange("p a h t -> p (a h t)"), psN[0:DA, 0:2 * HA * NS], ACT.Copy).then_inc(n_copied, 1)
                    act.wait_ge(max_ready, g + 1)
                    a.activation(s[:], s[:], ACT.Exp, scale=SC, bias=nm[:], accum_out=l[:])
                    a.drain().then_inc(p_ready, 1)
                    a.activation(ll[:], l[:], ACT.Ln)
                    act.wait_ge(p_turned, g + 1)
                    a.activation(pT[:], psT[:, 0, 0], ACT.Copy)
                    a.activation(pnT[:], psT[0:NS, 0, 1], ACT.Copy)
                    a.drain().then_inc(p_copied, 1)

            @block.vector
            def _(dve):
                v = nc.vector
                dve.sem_inc(q_used, RING)
                dve.wait_ge(mask_loaded, 16)
                for g in range(GA):
                    dve.wait_ge(kv_loaded[g], 16 * DEC_B)
                    with dve.Fori(0, DEC_B // RING) as i:
                        for r in range(RING):
                            b = i * RING + r
                            dve.wait_ge(q_loaded[r], 16 * (g * (DEC_B // RING) + i + 1))
                            k = kv[g][:, bass.ds(b, 1), :, 0:AW].rearrange("p a t c -> p (a t) c")
                            if g == 0:
                                k = k.to_broadcast([P, DEC_T, AW])
                            v.tensor_tensor(prod[:].rearrange("p (t h) d -> p t (h d)", t=DEC_T), qb[:, r], k, ALU.mult)
                            v.drain().then_inc(q_used, 1)
                            v.reduce_sum(S[:, :, bass.ds(b, 1), :].rearrange("p h a t -> p (a t) h"),
                                         prod[:].rearrange("p (t h) d -> p t h d", t=DEC_T), AX.X)
                            v.drain()
                    v.drain().then_inc(dots_done, 1)
                    dve.wait_ge(s_turned, g + 1)
                    v.tensor_tensor(s[:, 0:P], psA[:, 0:P], mk[:, g, 0:P], ALU.add)
                    v.tensor_tensor(s[:, P:P + NS], psB[:, 0:NS], mk[:, g, P:P + NS], ALU.add)
                    v.drain()
                    v.reduce_max(mx[:], s[:], AX.X)
                    v.drain()
                    v.tensor_scalar_mul(nm[:], mx[:], -SC).then_inc(max_ready, 1)
                    dve.wait_ge(p_copied, g + 1)
                    v.reciprocal(rl[:], l[:])
                    v.tensor_tensor(o[:, g, DA:DA + 1], ll[:], nm[:], ALU.subtract)
                    dve.wait_ge(o_summed, g + 1)
                    v.tensor_copy(oT[:], psO[0:DA, 0:P])
                    v.drain()
                    v.tensor_tensor(oT[:], psO2[0:DA, 0:P], oT[:], ALU.add).then_inc(oT_ready, 1)
                    dve.wait_ge(o_turned, g + 1)
                    v.tensor_scalar(o[:, g, 0:DA], psR[:, 0:DA], rl[:], None, ALU.mult)
                    v.drain().then_inc(o_ready, 1)

            @block.tensor
            def _(pe):
                T, M = nc.tensor.transpose, nc.tensor.matmul
                pe.wait_ge(new_loaded, 48)
                for g in range(GA):
                    if g:
                        pe.wait_ge(o_ready, g)
                    for a in range(2):
                        for h in range(HA):
                            last = T(psN[0:DA, (a * HA + h) * NS:(a * HA + h + 1) * NS], new[:, a, g, h * DA:(h + 1) * DA], ident[0:NS, 0:NS])
                    last.then_inc(n_turned, 1)
                    pe.wait_ge(n_copied, g + 1)
                    for h in range(HA):
                        M(psB[NS * h:NS * h + NS, 0:NS], nT[:, 0, h], nT[:, 1, h], start=True, stop=True)
                    pe.wait_ge(dots_done, g + 1)
                    T(psA[:, 0:P], S[:].rearrange("p h b t -> p (h b t)"), ident).then_inc(s_turned, 1)
                    pe.wait_ge(p_ready, g + 1)
                    T(psT[:, 0, 0], s[:, 0:P], ident)
                    T(psT[0:NS, 0, 1], s[:, P:P + NS], ident).then_inc(p_turned, 1)
                    pe.wait_ge(p_copied, g + 1)
                    for h in range(HA):
                        for b in range(DEC_B):
                            for t in range(DEC_T):
                                r = (h * DEC_B + b) * DEC_T + t
                                M(psO[0:DA, r:r + 1], kv[g][:, b, 0 if g == 0 else t, AW + h * DA:AW + (h + 1) * DA], pT[:, r:r + 1],
                                  start=True, stop=True)
                        last = M(psO2[0:DA, NS * h:NS * h + NS], new[:, 2, g, h * DA:(h + 1) * DA], pnT[:, NS * h:NS * h + NS], start=True, stop=True)
                    last.then_inc(o_summed, 1)
                    pe.wait_ge(oT_ready, g + 1)
                    T(psR[:, 0:DA], oT[:], ident[0:DA, 0:DA]).then_inc(o_turned, 1)


def merge_heads(nc, tag, ol, h_b, z, g_row, out):
    SLOTS = 3
    OW = HA * (DA + 1)
    with ExitStack() as ctx:
        sb = lambda n, s: ctx.enter_context(nc.sbuf_tensor(f"{tag}_{n}", s, F32))
        sem = Sems(nc, ctx, tag)
        ot = sb("ot", [P, SLOTS, GA, HA, DA + 1])
        hb, og = sb("hb", [P, SLOTS, HB, DB]), sb("og", [P, SLOTS, BW])
        mx, w, ws = sb("mx", [P, HA]), sb("w", [P, HA, GA]), sb("ws", [P, HA])
        hsq, ss, sd = sb("hsq", [P, BW]), sb("ss", [P, HB]), sb("sd", [P, HB])
        e, u = sb("e", [P, BW]), sb("u", [P, HA, DA])
        res, eps = sb("res", [P, SLOTS, MIX]), sb("eps", [P, 1])
        loaded, stored, res_free = sem("loaded", SLOTS), sem("stored"), sem("res_free")
        tile_done, w_ready, w_exp, e_ready, ss_ready, sd_ready = (
            sem(n) for n in ("tile_done", "w_ready", "w_exp", "e_ready", "ss_ready", "sd_ready"))
        with nc.Block() as block:

            @block.sync
            def _(sp):
                with sp.Fori(0, TILES // SLOTS) as i:
                    for j in range(SLOTS):
                        row = bass.ds((i * SLOTS + j) * P, P)
                        sp.wait_ge(tile_done, i * SLOTS + j + 1)
                        for g in range(GA):
                            sp.dma_start(ot[:, j, g].rearrange("p h d -> p (h d)"), ol[g][row, :]).then_inc(loaded[j], 16)
                        sp.dma_start(hb[:, j].rearrange("p h d -> p (h d)"), h_b[row, :]).then_inc(loaded[j], 16)
                        sp.dma_start(og[:, j], z[row, OFF_OG:OFF_OG + BW]).then_inc(loaded[j], 16)

            @block.scalar
            def _(act):
                a = nc.scalar
                with act.Fori(0, TILES // SLOTS) as i:
                    for j in range(SLOTS):
                        t = i * SLOTS + j
                        act.wait_ge(loaded[j], 80 * i + 80)
                        act.wait_ge(tile_done, t + SLOTS)
                        a.activation(e[:], og[:, j], ACT.Tanh, scale=0.5)
                        a.drain().then_inc(e_ready, 1)
                        act.wait_ge(w_ready, t + 1)
                        a.activation(w[:], w[:], ACT.Exp).then_inc(w_exp, 1)
                        act.wait_ge(ss_ready, t + 1)
                        a.activation(sd[:], ss[:], ACT.Ln, scale=1.0 / DB, bias=eps[:])
                        a.drain()
                        a.activation(sd[:], sd[:], ACT.Exp, scale=-0.5).then_inc(sd_ready, 1)

            @block.vector
            def _(dve):
                v = nc.vector
                v.memset(eps[:], EPS)
                dve.sem_inc(tile_done, SLOTS)
                with dve.Fori(0, TILES // SLOTS) as i:
                    for j in range(SLOTS):
                        t = i * SLOTS + j
                        dve.wait_ge(loaded[j], 80 * i + 80)
                        lse = ot[:, j, :, :, DA].rearrange("p g h -> p h g")
                        h2 = hb[:, j].rearrange("p h d -> p (h d)")
                        v.reduce_max(mx[:], lse, AX.X)
                        v.tensor_tensor(hsq[:], h2, h2, ALU.mult)
                        v.drain()
                        v.tensor_tensor(w[:], lse, mx[:].unsqueeze(2).to_broadcast([P, HA, GA]), ALU.subtract)
                        v.reduce_sum(ss[:], hsq[:].rearrange("p (h d) -> p h d", h=HB), AX.X)
                        v.drain().then_inc(w_ready, 1)
                        v.drain().then_inc(ss_ready, 1)
                        dve.wait_ge(e_ready, t + 1)
                        v.tensor_scalar(e[:], e[:], 1.0, 0.5, ALU.add, ALU.mult)
                        v.drain()
                        v.tensor_tensor(e[:], e[:], g_row, ALU.mult)
                        v.drain()
                        v.tensor_tensor(e[:], e[:], h2, ALU.mult)
                        dve.wait_ge(w_exp, t + 1)
                        v.reduce_sum(ws[:], w[:], AX.X)
                        v.drain()
                        v.reciprocal(ws[:], ws[:])
                        v.drain()
                        dve.wait_ge(res_free, t + 1)
                        v.tensor_tensor(w[:], w[:], ws[:].unsqueeze(2).to_broadcast([P, HA, GA]), ALU.mult)
                        v.drain()
                        o_a = res[:, j, 0:AW].rearrange("p (h d) -> p h d", h=HA)
                        wide = lambda g: w[:, :, g:g + 1].to_broadcast([P, HA, DA])
                        v.tensor_tensor(o_a, ot[:, j, 0, :, 0:DA], wide(0), ALU.mult)
                        for g in range(1, GA):
                            v.tensor_tensor(u[:], ot[:, j, g, :, 0:DA], wide(g), ALU.mult)
                            v.drain()
                            v.tensor_tensor(o_a, o_a, u[:], ALU.add)
                            v.drain()
                        dve.wait_ge(sd_ready, t + 1)
                        v.tensor_tensor(res[:, j, AW:MIX].rearrange("p (h d) -> p h d", h=HB), e[:].rearrange("p (h d) -> p h d", h=HB),
                                        sd[:].unsqueeze(2).to_broadcast([P, HB, DB]), ALU.mult)
                        v.drain().then_inc(tile_done, 1)

            @block.gpsimd
            def _(pool):
                pool.sem_inc(res_free, SLOTS)
                with pool.Fori(0, TILES // SLOTS) as i:
                    for j in range(SLOTS):
                        t = i * SLOTS + j
                        pool.wait_ge(tile_done, t + SLOTS + 1)
                        pool.dma_start(out[bass.ds(t * P, P), :], res[:, j]).then_inc(stored, 16)
                        pool.wait_ge(stored, 16 * t + 16)
                        pool.sem_inc(res_free, 1)


def transpose_rows(nc, tag, src, kc, ident, xT, lo):
    SLOTS = 3
    with ExitStack() as ctx:
        sem = Sems(nc, ctx, tag)
        rows = ctx.enter_context(nc.sbuf_tensor(f"{tag}_rows", [P, SLOTS, kc * P], F32))
        ps = ctx.enter_context(nc.psum_tensor(f"{tag}_ps", [P, SLOTS, KD, P], F32))
        row_loaded = sem("row_loaded", SLOTS)
        turned, copied = sem("turned"), sem("copied")
        with nc.Block() as block:

            @block.sync
            def _(sp):
                with sp.Fori(0, TILES // SLOTS) as i:
                    for j in range(SLOTS):
                        sp.wait_ge(turned, i * SLOTS + j + 1)
                        sp.dma_start(rows[:, j, :], src[bass.ds((i * SLOTS + j) * P, P), :]).then_inc(row_loaded[j], 16)

            @block.tensor
            def _(pe):
                pe.sem_inc(turned, SLOTS)
                with pe.Fori(0, TILES // SLOTS) as i:
                    for j in range(SLOTS):
                        pe.wait_ge(row_loaded[j], 16 * i + 16)
                        pe.wait_ge(copied, i * SLOTS + j + 1)
                        for k in range(kc):
                            last = nc.tensor.transpose(ps[:, j, k, :], rows[:, j, k * P:(k + 1) * P], ident)
                        last.then_inc(turned, 1)

            @block.vector
            def _(dve):
                dve.sem_inc(copied, SLOTS)
                with dve.Fori(0, TILES // SLOTS) as i:
                    for j in range(SLOTS):
                        cols = bass.ds((i * SLOTS + j) * P, P)
                        dve.wait_ge(turned, i * SLOTS + j + 1 + SLOTS)
                        nc.vector.tensor_copy(xT[:, :, cols], ps[:, j, 0:kc])
                        nc.vector.drain()
                        nc.vector.tensor_tensor(lo[:, :, cols], ps[:, j, 0:kc], xT[:, :, cols].bitcast(F32), ALU.subtract)
                        nc.vector.drain().then_inc(copied, 1)


GELU_C = (2.0 / np.pi) ** 0.5


def compress(nc, tag, pool_kv, pages, z, w1, w2, pe, ident, KC, KP, VC):
    GP = 4
    CP = P // STRIDE
    NPG = PAST // PAGE // GP
    with ExitStack() as ctx:
        sb = lambda n, s: ctx.enter_context(nc.sbuf_tensor(f"{tag}_{n}", s, F32))
        pb = lambda n, s: ctx.enter_context(nc.psum_tensor(f"{tag}_{n}", s, F32))
        sem = Sems(nc, ctx, tag)
        w1t = sb("w1", [P, 2, CBLK, P])
        w2t = sb("w2", [P, 2, P])
        pet, peT = sb("pe", [CBLK, 2, KVH, DC]), sb("peT", [P, 2, CBLK])
        pbias = sb("pbias", [P, 2])
        pg = sb("pg", [P, 2, GP, 2 * KVW])
        X = sb("X", [P, 2, STRIDE, P])
        x, u, e, g = (sb(n, [P, 2, P]) for n in ("x", "u", "e", "g"))
        psT, psH = pb("psT", [P, 2, 2, GP * P]), pb("psH", [P, 2, P])
        psK, psV = pb("psK", [P, 512]), pb("psV", [P, 512])
        w_loaded, w_clear, page_loaded = sem("w_loaded"), sem("w_clear"), sem("page_loaded", 2)
        pe_turned, pe_copied, bias_done, bias_read = sem("pe_turned"), sem("pe_copied"), sem("bias_done"), sem("bias_read")
        turned, copied = sem("turned"), sem("copied", 2)
        hid_done, cubic, e_ready, g_ready, kv_done, kv_read = (
            sem(n) for n in ("hid_done", "cubic", "e_ready", "g_ready", "kv_done", "kv_read"))
        with nc.Block() as block:

            @block.scalar
            def _(act):
                a = nc.scalar
                act.wait_ge(w_clear, 1)
                for kv in range(2):
                    for h in range(KVH):
                        d = slice(h * DC, (h + 1) * DC)
                        act.dma_start(w1t[d, kv, :, d], w1[kv].rearrange("r d e -> d r e")).then_inc(w_loaded, 16)
                        act.dma_start(w2t[d, kv, d], w2[kv]).then_inc(w_loaded, 16)
                        act.dma_start(pet[:, kv, h], pe[kv]).then_inc(w_loaded, 16)

                def batch(u0, n_groups, b):
                    for q in range(n_groups):
                        act.wait_ge(turned, u0 + q + 3)
                        a.activation(X[:, 1, :, CP * GP * q:CP * GP * (q + 1)].rearrange("p r c -> p c r"),
                                     psT[:, q % 2, 1].rearrange("p (c r) -> p c r", r=STRIDE), ACT.Copy).then_inc(copied[1], 1)
                    act.wait_ge(cubic, b + 1)
                    a.activation(e[:], u[:], ACT.Tanh, scale=GELU_C).then_inc(e_ready, 1)

                with act.Fori(0, DEC_B) as b:
                    batch(b * NPG, NPG, b)
                batch(DEC_B * NPG, PT // GP, DEC_B)

            @block.sync
            def _(sp):

                with sp.Fori(0, DEC_B) as b:
                    for q in range(NPG):
                        sp.wait_ge(turned, b * NPG + q + 1)
                        for a in range(GP):
                            page = sp.value_load(pages[0:1, bass.ds(b * (NPG * GP) + q * GP + a, 1)], min_val=0, max_val=pool_kv.shape[0] - 1)
                            sp.dma_start(pg[:, q % 2, a], pool_kv[bass.ds(page, 1)].rearrange("o p c -> p (o c)")).then_inc(page_loaded[q % 2], 16)
                for q in range(PT // GP):
                    sp.wait_ge(turned, DEC_B * NPG + q + 1)
                    for a in range(GP):
                        t = q * GP + a
                        sp.dma_start(pg[:, q % 2, a], z[t * P:(t + 1) * P, OFF_CMP:OFF_CMP + 2 * KVW]).then_inc(page_loaded[q % 2], 16)

            @block.tensor
            def _(pe_):
                T, M = nc.tensor.transpose, nc.tensor.matmul
                pe_.wait_ge(w_loaded, 16 * 12)
                for kv in range(2):
                    last = T(psK[:, kv * CBLK:(kv + 1) * CBLK], pet[:, kv].rearrange("r h d -> r (h d)"), ident[0:CBLK, 0:CBLK])
                last.then_inc(pe_turned, 1)
                pe_.wait_ge(pe_copied, 1)
                for kv in range(2):
                    for r in range(CBLK):
                        last = M(psV[:, kv:kv + 1], w1t[:, kv, r], peT[:, kv, r:r + 1], start=(r == 0), stop=(r == CBLK - 1))
                last.then_inc(bias_done, 1)
                pe_.wait_ge(bias_read, 1)
                pe_.sem_inc(turned, 2)

                def batch(u0, n_groups, b, n, half, sample):
                    for q in range(n_groups):
                        pe_.wait_ge(page_loaded[q % 2], half(q))
                        pe_.wait_ge(copied[0], u0 + q + 1)
                        pe_.wait_ge(copied[1], u0 + q + 1)
                        for kv in range(2):
                            for a in range(GP):
                                last = T(psT[:, q % 2, kv, a * P:(a + 1) * P], pg[:, q % 2, a, kv * KVW:(kv + 1) * KVW], ident)
                        last.then_inc(turned, 1)
                    pe_.wait_ge(copied[0], u0 + n_groups + 2)
                    pe_.wait_ge(copied[1], u0 + n_groups + 2)
                    for kv in range(2):
                        for r in range(CBLK):
                            last = M(psH[:, kv, 0:n], w1t[:, kv, r], X[:, kv, r % STRIDE, r // STRIDE:r // STRIDE + n],
                                     start=(r == 0), stop=(r == CBLK - 1))
                    last.then_inc(hid_done, 1)
                    pe_.wait_ge(g_ready, b + 1)
                    pe_.wait_ge(kv_read, b + 1)
                    if sample:
                        M(psK[:, 0:n], w2t[:, 0], g[:, 0, 0:n], start=True, stop=True)
                    for half in range(0 if sample else 2):
                        for h in range(KVH):
                            M(psK[half * DC:(half + 1) * DC, h * P:h * P + n], w2t[:, 0, h * DC:(h + 1) * DC], g[:, 0, 0:n], start=True, stop=True)
                    M(psV[0:n, 0:KVW], g[:, 1, 0:n], w2t[:, 1], start=True, stop=True).then_inc(kv_done, 1)

                with pe_.Fori(0, DEC_B) as b:
                    batch(b * NPG, NPG, b, NCMP_S, lambda q: (b * (NPG // 2) + q // 2 + 1) * (16 * GP), True)
                batch(DEC_B * NPG, PT // GP, DEC_B, NCMP_P, lambda q: (DEC_B * NPG // 2 + q // 2 + 1) * (16 * GP), False)

            @block.vector
            def _(dve):
                v = nc.vector
                v.memset(w1t[:], 0.0)
                v.memset(w2t[:], 0.0)
                v.drain().then_inc(w_clear, 1)
                v.memset(g[:], 0.0)
                v.memset(KP, 0.0)
                dve.wait_ge(pe_turned, 1)
                v.tensor_copy(peT[:].rearrange("p a r -> p (a r)"), psK[:, 0:2 * CBLK]).then_inc(pe_copied, 1)
                dve.wait_ge(bias_done, 1)
                v.tensor_copy(pbias[:], psV[:, 0:2])
                v.drain().then_inc(bias_read, 1)
                dve.sem_inc(copied[0], 2)
                dve.sem_inc(copied[1], 2)
                dve.sem_inc(kv_read, 1)

                def batch(u0, n_groups, b, at, n):
                    for q in range(n_groups):
                        dve.wait_ge(turned, u0 + q + 3)
                        v.tensor_copy(X[:, 0, :, CP * GP * q:CP * GP * (q + 1)].rearrange("p r c -> p c r"),
                                      psT[:, q % 2, 0].rearrange("p (c r) -> p c r", r=STRIDE)).then_inc(copied[0], 1)
                    dve.wait_ge(hid_done, b + 1)
                    c = slice(0, n)
                    for kv in range(2):
                        v.tensor_scalar(x[:, kv, c], psH[:, kv, c], pbias[:, kv:kv + 1], None, ALU.add)
                    v.drain()
                    v.tensor_tensor(u[:, :, c], x[:, :, c], x[:, :, c], ALU.mult)
                    v.drain()
                    v.tensor_scalar(u[:, :, c], u[:, :, c], 0.044715, 1.0, ALU.mult, ALU.add)
                    v.drain()
                    v.tensor_tensor(u[:, :, c], u[:, :, c], x[:, :, c], ALU.mult)
                    v.drain().then_inc(cubic, 1)
                    dve.wait_ge(e_ready, b + 1)
                    v.tensor_scalar(e[:, :, c], e[:, :, c], 1.0, 0.5, ALU.add, ALU.mult)
                    v.drain()
                    v.tensor_tensor(g[:, :, c], e[:, :, c], x[:, :, c], ALU.mult).then_inc(g_ready, 1)
                    dve.wait_ge(kv_done, b + 1)
                    if n == NCMP_S:
                        v.tensor_copy(KC[:, at, c].rearrange("p o c -> p (o c)"), psK[:, c])
                    else:
                        v.tensor_copy(KP[:, :, c], psK[:, 0:KVH * P].rearrange("p (h c) -> p h c", h=KVH)[:, :, c])
                    v.tensor_copy(VC[0:n, at, :].rearrange("p o c -> p (o c)"), psV[0:n, 0:KVW])
                    v.drain().then_inc(kv_read, 1)

                v.memset(u[:], 0.0)
                v.memset(x[:], 0.0)
                v.drain()
                with dve.Fori(0, DEC_B) as b:
                    batch(b * NPG, NPG, b, bass.ds(b, 1), NCMP_S)
                batch(DEC_B * NPG, PT // GP, DEC_B, slice(DEC_B, DEC_B + 1), NCMP_P)


def gate_sigmoid(nc, tag, src, dst):
    with ExitStack() as ctx:
        sem = Sems(nc, ctx, tag)
        loaded, e_ready = sem("loaded"), sem("e_ready")
        with nc.Block() as block:

            @block.sync
            def _(sp):
                sp.dma_start(dst, src).then_inc(loaded, 16)

            @block.scalar
            def _(act):
                act.wait_ge(loaded, 16)
                nc.scalar.activation(dst, dst, ACT.Tanh, scale=0.5).then_inc(e_ready, 1)

            @block.vector
            def _(dve):
                dve.wait_ge(e_ready, 1)
                nc.vector.tensor_scalar(dst, dst, 1.0, 0.5, ALU.add, ALU.mult)


def nsa_prompt(nc, tag, z, qk, cmask, causal, early, KP, VC, gates, ident, out):
    SC = DC ** -0.5
    WT = WIN // P
    UN = GC
    SELW, WINW = SEQ, (WT + 1) * P
    with ExitStack() as ctx:
        sb = lambda n, s: ctx.enter_context(nc.sbuf_tensor(f"{tag}_{n}", s, F32))
        pb = lambda n, s: ctx.enter_context(nc.psum_tensor(f"{tag}_{n}", s, F32))
        sem = Sems(nc, ctx, tag)
        krow = sb("krow", [P, 2, PT, KVH, 2, DC])
        vrow = sb("vrow", [P, 2, PT, KVW])
        fr = lambda n, s: ctx.enter_context(nc.sbuf_tensor(f"{tag}_{n}", s, FR))
        kT, cT = fr("kT", [P, 2, 2, KVH, SEQ]), fr("cT", [P, 2, KVH, NCMP_P + 1])
        qt = sb("qt", [P, 2, 2, 2, DC])
        q2 = sb("q2", [P, 2, P])
        zero = sb("zero", [P, 2, P])
        qT = fr("qT", [P, 2, 2, P])
        p_ = sb("p", [P, 2, SELW + WINW + DC])
        mx, nm, l, rl, w = (sb(n, [P, 2, 3]) for n in ("mx", "nm", "l", "rl", "w"))
        pT = sb("pT", [P, 2, 4, P])
        o3, ot = sb("o3", [P, 3, DC]), sb("ot", [P, 2, GC * DC])
        psS, psW = pb("psS", [P, SELW]), pb("psW", [P, 1024])
        psQ, psP, psO = pb("psQ", [P, 512]), pb("psP", [P, 2, 4 * P]), pb("psO", [P, 3, DC])
        kv_loaded, k_turned, k_copied = sem("kv_loaded"), sem("k_turned"), sem("k_copied")
        q_loaded, q_turned, q_copied, q_split = sem("q_loaded", 2), sem("q_turned"), sem("q_copied"), sem("q_split")
        scored, max_ready, p_ready, o_done, unit_done = (sem(n) for n in ("scored", "max_ready", "p_ready", "o_done", "unit_done"))
        p_turned, p_copied, p_used, stored = sem("p_turned"), sem("p_copied", 2), sem("p_used"), sem("stored", 2)
        CM = SELW + WINW
        runs = [(i, kv) for i in range(PT) for kv in range(KVH)]

        def groups(i):
            pieces = [(0, a, a * P, P) for a in range(i + 1)]
            pieces += [(1, a, SELW + (a - max(0, i - WT)) * P, P) for a in range(max(0, i - WT), i + 1)]
            pieces.append((2, 0, CM, NCMP_P))
            cuts = list(range(0, len(pieces), 4)) + [len(pieces)]
            if len(pieces) % 4 == 1 and len(pieces) > 1:
                cuts[-2] -= 1
            return [pieces[a:b] for a, b in zip(cuts, cuts[1:])]

        done_groups, done_by, total, by = {}, {}, 0, [0, 0]
        for r, (i, kv) in enumerate(runs):
            done_groups[r], done_by[r] = total, tuple(by)
            n = len(groups(i))
            total += UN * n
            by = [by[0] + UN * ((n + 1) // 2), by[1] + UN * (n // 2)]

        def by_act(gs):
            return (len(gs) + 1) // 2

        def copies(r, f, k):
            return done_by[r][k % 2] + f * ((len(groups(runs[r][0])) + 1 - k % 2) // 2) + k // 2 + 1

        def copy_group(eng, copy, pT, psP, gs, r, f, u, k):
            eng.wait_ge(p_turned, done_groups[r] + f * len(gs) + k + 1)
            if k >= 2:
                eng.wait_ge(p_used, (done_groups[r] - r * UN) + f * (len(gs) - 1) + k - 1)
            full = len(gs[k]) - (gs[k][-1][0] == 2)
            if full:
                copy(pT[:, k % 2, 0:full], psP[:, k % 2, 0:full * P].rearrange("p (c t) -> p c t", t=P))
            if gs[k][-1][0] == 2:
                copy(pT[0:NCMP_P, k % 2, full], psP[0:NCMP_P, k % 2, full * P:(full + 1) * P])
            eng.drain().then_inc(p_copied[k % 2], 1)

        with nc.Block() as block:

            @block.sync
            def _(sp):
                v = lambda t, c: t[0:SEQ, c:c + KVW].rearrange("(a p) c -> p a c", p=P)
                for br in range(2):
                    for twice in range(2):
                        for kv in range(KVH):
                            sp.dma_start(krow[:, br, :, kv, twice], qk[0:SEQ, CQ + br * KVW + kv * DC:CQ + br * KVW + (kv + 1) * DC]
                                         .rearrange("(a p) c -> p a c", p=P)).then_inc(kv_loaded, 16)
                sp.dma_start(vrow[:, 0], v(z, OFF_SEL + KVW)).then_inc(kv_loaded, 16)
                sp.dma_start(vrow[:, 1], v(z, OFF_WIN + KVW)).then_inc(kv_loaded, 16)
                twice = lambda rows: rows.unsqueeze(1).to_broadcast([P, 2, DC])
                for r, (i, kv) in enumerate(runs):
                    with sp.Fori(0, UN // 2) as m:
                        for j in range(2):
                            f = 2 * m + j
                            sp.wait_ge(q_turned, r * UN + f + 1)
                            col = bass.ds((kv * GC + f) * DC, DC)
                            sp.dma_start(qt[:, j, 0], twice(z[i * P:(i + 1) * P, col])).then_inc(q_loaded[j], 16)
                            sp.dma_start(qt[:, j, 1], twice(qk[i * P:(i + 1) * P, col])).then_inc(q_loaded[j], 16)

            @block.tensor
            def _(pe):
                T, M = nc.tensor.transpose, nc.tensor.matmul
                pe.wait_ge(kv_loaded, 16 * 10)
                n = 0
                for br in range(2):
                    for kv in range(KVH):
                        for a in range(0, PT, 4):
                            if n:
                                pe.wait_ge(k_copied, n)
                            for c in range(4):
                                last = T(psQ[:, c * P:(c + 1) * P], krow[:, br, a + c, kv].rearrange("p w d -> p (w d)"), ident)
                            last.then_inc(k_turned, 1)
                            n += 1
                pe.wait_ge(k_copied, n)
                pe.sem_inc(q_turned, 2)

                def turn_queries(u, j):
                    pe.wait_ge(q_loaded[j], 16 * (u - j) + 32)
                    pe.wait_ge(q_copied, u + 1)
                    for a in range(2):
                        last = T(psQ[:, a * P:(a + 1) * P], qt[:, j, a].rearrange("p w d -> p (w d)"), ident)
                    last.then_inc(q_turned, 1)

                turn_queries(0, 0)
                for r, (i, kv) in enumerate(runs):
                    gs = groups(i)
                    w0 = max(0, i - WT)

                    def score(out, q, hi, lo):
                        M(out, q, hi, start=True, stop=False)
                        return M(out, q, lo, start=False, stop=True)

                    def front(f, j):
                        u = r * UN + f
                        pe.wait_ge(q_split, u + 1)
                        pe.wait_ge(p_ready, u + 1)
                        for c in range(0, (i + 1) * P, 512):
                            n = min(512, (i + 1) * P - c)
                            score(psS[:, c:c + n], qT[:, j, 1], kT[:, 0, 0, kv, c:c + n], kT[:, 1, 0, kv, c:c + n])
                        for c in range(0, (i + 1 - w0) * P, 512):
                            n = min(512, (i + 1 - w0) * P - c)
                            k = slice(w0 * P + c, w0 * P + c + n)
                            score(psW[:, c:c + n], qT[:, j, 1], kT[:, 0, 1, kv, k], kT[:, 1, 1, kv, k])
                        score(psW[:, WINW:WINW + NCMP_P + 1], qT[:, j, 0], cT[:, 0, kv], cT[:, 1, kv]).then_inc(scored, 1)
                        if not (isinstance(f, int) and u == len(runs) * UN - 1):
                            turn_queries(u + 1, 1 - j)

                    def back(f, j):
                        u = r * UN + f
                        pe.wait_ge(p_ready, u + 2)
                        pe.wait_ge(unit_done, u + 1)

                        def turn(k):
                            if k >= 2:
                                pe.wait_ge(p_copied[k % 2], copies(r, f, k - 2))
                            for c, (br, a, col, n) in enumerate(gs[k]):
                                last = T(psP[0:n, k % 2, c * P:(c + 1) * P], p_[:, j, col:col + n], ident)
                            last.then_inc(p_turned, 1)

                        def product(k):
                            pe.wait_ge(p_copied[k % 2], copies(r, f, k))
                            for c, (br, a, col, n) in enumerate(gs[k]):
                                first = a == (0 if br != 1 else w0)
                                end = a == (0 if br == 2 else i)
                                rhs = VC[0:n, DEC_B, kv * DC:(kv + 1) * DC] if br == 2 else vrow[:, br, a, kv * DC:(kv + 1) * DC]
                                last = M(psO[:, br], pT[0:n, k % 2, c], rhs, start=first, stop=end)
                            if k == len(gs) - 1:
                                last.then_inc(o_done, 1)
                            else:
                                last.then_inc(p_used, 1)

                        for k in range(len(gs)):
                            turn(k)
                            if k:
                                product(k - 1)
                        product(len(gs) - 1)

                    overlapped(pe, UN, front, back)

            @block.scalar
            def _(act):
                a = nc.scalar
                act.sem_inc(q_copied, 1)
                act.sem_inc(p_ready, 1)

                def copy_queries(u):
                    act.wait_ge(q_turned, u + 3)
                    if not isinstance(u, int) or u > 0:
                        act.wait_ge(q_split, u)
                    a.activation(q2[:].rearrange("p a t -> p (a t)"), psQ[:, 0:2 * P], ACT.Copy).then_inc(q_copied, 1)

                copy_queries(0)
                for r, (i, kv) in enumerate(runs):
                    gs = groups(i)
                    w0 = max(0, i - WT)

                    def front(f, j):
                        if not (isinstance(f, int) and r * UN + f == len(runs) * UN - 1):
                            copy_queries(r * UN + f + 1)
                        if isinstance(f, int) and f == 0:
                            exps(f, j)

                    def exps(f, j):
                        u = r * UN + f
                        act.wait_ge(max_ready, u + 1)
                        for br, (src, to, n) in enumerate(((psS[:, 0:(i + 1) * P], 0, (i + 1) * P),
                                                           (psW[:, 0:(i + 1 - w0) * P], SELW, (i + 1 - w0) * P),
                                                           (psW[:, WINW:WINW + NCMP_P], CM, NCMP_P))):
                            a.activation(p_[:, j, to:to + n], src, ACT.Exp, scale=SC, bias=nm[:, j, br:br + 1], accum_out=l[:, j, br:br + 1])
                        a.drain().then_inc(p_ready, 1)

                    def back(f, j):
                        for k in range(by_act(gs)):
                            copy_group(act, lambda to, x: a.activation(to, x, ACT.Copy), pT, psP, gs, r, f, r * UN + f, k)
                        if not (isinstance(f, int) and f == UN - 1):
                            exps(f + 1, 1 - j)

                    overlapped(act, UN, front, back)

            @block.vector
            def _(dve):
                v = nc.vector
                dve.sem_inc(unit_done, 1)

                def split(hi, lo, x):
                    v.tensor_copy(hi, x)
                    v.drain()
                    v.tensor_tensor(lo, x, hi.bitcast(F32), ALU.subtract)

                split(cT[:, 0], cT[:, 1], KP)
                n = 0
                for br in range(2):
                    for kv in range(KVH):
                        for a in range(0, PT, 4):
                            n += 1
                            dve.wait_ge(k_turned, n)
                            split(kT[:, 0, br, kv, a * P:(a + 4) * P], kT[:, 1, br, kv, a * P:(a + 4) * P], psQ[:, 0:4 * P])
                            v.drain().then_inc(k_copied, 1)
                for r, (i, kv) in enumerate(runs):
                    gs = groups(i)
                    w0 = max(0, i - WT)

                    def front(f, j):
                        u = r * UN + f
                        dve.wait_ge(scored, u + 1)
                        s, t = psS[:, i * P:(i + 1) * P], psW[:, (i - w0) * P:(i + 1 - w0) * P]
                        v.tensor_tensor(s, s, causal, ALU.add)
                        v.tensor_tensor(t, t, causal, ALU.add)
                        if i >= WT:
                            v.tensor_tensor(psW[:, 0:P], psW[:, 0:P], early, ALU.add)
                        c = psW[:, WINW:WINW + NCMP_P]
                        v.tensor_tensor(c, c, cmask[:, i], ALU.add)
                        v.drain()
                        v.reduce_max(mx[:, j, 0:1], psS[:, 0:(i + 1) * P], AX.X)
                        v.reduce_max(mx[:, j, 1:2], psW[:, 0:(i + 1 - w0) * P], AX.X)
                        v.reduce_max(mx[:, j, 2:3], c, AX.X)
                        v.drain()
                        v.tensor_scalar(nm[:, j], mx[:, j], -1e20, -SC, ALU.max, ALU.mult).then_inc(max_ready, 1)

                    def back(f, j):
                        u = r * UN + f
                        dve.wait_ge(p_ready, u + 2)
                        for k in range(by_act(gs), len(gs)):
                            copy_group(dve, v.tensor_copy, pT, psP, gs, r, f, u, k)
                        v.tensor_scalar_max(rl[:, j], l[:, j], 1e-30)
                        v.drain()
                        v.reciprocal(rl[:, j], rl[:, j])
                        v.drain()
                        gate = gates[:, i, bass.ds(kv * GC + f, 1)].rearrange("p o b -> p (o b)")
                        v.tensor_tensor(w[:, j, 0:2], rl[:, j, 0:2], gate[:, 1:3], ALU.mult)
                        v.tensor_tensor(w[:, j, 2:3], rl[:, j, 2:3], gate[:, 0:1], ALU.mult)
                        v.drain()
                        dve.wait_ge(o_done, u + 1)
                        v.tensor_tensor(o3[:], psO[:], w[:, j].unsqueeze(2).to_broadcast([P, 3, DC]), ALU.mult)
                        v.drain().then_inc(unit_done, 1)
                        v.reduce_sum(ot[:, r % 2, bass.ds(f * DC, DC)], o3[:].rearrange("p b d -> p d b"), AX.X)

                    if r >= 2:
                        dve.wait_ge(stored[r % 2], 16 * (r // 2))
                    overlapped(dve, UN, front, back)
                    v.drain().then_inc(k_copied, 1)

            @block.gpsimd
            def _(pool):

                def split_queries(u, j):
                    pool.wait_ge(q_copied, u + 2)
                    nc.gpsimd.tensor_tensor(qT[:, j], q2[:], zero[:], ALU.subtract)
                    nc.gpsimd.drain()
                    nc.gpsimd.tensor_tensor(qT[DC:P, j], q2[DC:P], qT[DC:P, j].bitcast(F32), ALU.subtract)
                    nc.gpsimd.drain().then_inc(q_split, 1)

                nc.gpsimd.memset(zero[:], 0.0)
                nc.gpsimd.drain()
                split_queries(0, 0)
                for r, (i, kv) in enumerate(runs):
                    with pool.Fori(0, UN // 2 - 1) as m:
                        split_queries(r * UN + 2 * m + 1, 1)
                        split_queries(r * UN + 2 * m + 2, 0)
                    split_queries(r * UN + UN - 1, 1)
                    if r < len(runs) - 1:
                        split_queries((r + 1) * UN, 0)
                    pool.wait_ge(k_copied, 2 * KVH * PT // 4 + r + 1)
                    pool.dma_start(out[i * P:(i + 1) * P, kv * GC * DC:(kv + 1) * GC * DC], ot[:, r % 2]).then_inc(stored[r % 2], 16)
                for j in range(2):
                    pool.wait_ge(stored[j], 16 * (len(runs) // 2))


def nsa_sample(nc, tag, z, qk, sel_pool, pages, win, KC, VC, gates, wslc, gsum, forced, new_mask, win_mask, ident, out):
    SC = DC ** -0.5
    PAIRS = DEC_B // 2
    NP, WP, G = PAST // PAGE, WIN // PAGE, 4
    STEPS, NG = NP + WP, (NP + WP) // G
    C2, S2, W2 = P, PAST + NS, WIN + NS
    Q4 = 4
    row = slice(SEQ, TOK)
    with ExitStack() as ctx:
        sb = lambda n, s: ctx.enter_context(nc.sbuf_tensor(f"{tag}_{n}", s, F32))
        pb = lambda n, s: ctx.enter_context(nc.psum_tensor(f"{tag}_{n}", s, F32))
        sem = Sems(nc, ctx, tag)
        kv = sb("kv", [P, 2, STEPS, 2, 2 * KVW])
        qn, kn = sb("qn", [NS, 2, GC, KVH, DC]), sb("kn", [NS, 2, KVW])
        vn = sb("vn", [NS, 2, KVW])
        QT, KN = sb("QT", [KVW, 2, DEC_B, GC * DEC_T]), sb("KN", [KVW, 2, NS])
        qp, kcp, vcp = sb("qp", [KVW, 2, 2, KVH, 32]), sb("kcp", [KVW, 2, P]), sb("vcp", [P, 2, KVW])
        kT = sb("kT", [KVW, 2, 2, P])
        sc, ss, sw = sb("sc", [P, C2]), sb("ss", [P, S2]), sb("sw", [P, W2])
        pcT, pT = sb("pcT", [P, P]), sb("pT", [P, 2, G, P])
        imp, x1, x2 = sb("imp", [P, NSLC]), sb("x1", [P, NSLC]), sb("x2", [P, NSLC])
        m8 = sb("m8", [P, 8])
        mx, nm, l, rl, w = (sb(n, [P, 3]) for n in ("mx", "nm", "l", "rl", "w"))
        o3, o = sb("o3", [P, 3, DC]), sb("o", [P, 2, DC])
        psK, psS = pb("psK", [KVW, 2, 4, P]), pb("psS", [P, 2, 512])
        psM = pb("psM", [P, 512])
        psP, psO = pb("psP", [P, 2, 512]), pb("psO", [P, 3, KVW])
        small_loaded, loaded = sem("small_loaded"), sem("loaded", 2)
        n_turned, n_copied, qp_ready, c_scored, c_max, c_exp, c_norm, c_turned, c_copied = (
            sem(n) for n in ("n_turned", "n_copied", "qp_ready", "c_scored", "c_max", "c_exp", "c_norm", "c_turned", "c_copied"))
        imp1, imp1_read, imp2 = sem("imp1"), sem("imp1_read"), sem("imp2")
        k_turned, k_copied, page_scored, group_read, new_scored = (
            sem(n) for n in ("k_turned", "k_copied", "page_scored", "group_read", "new_scored"))
        max_ready, p_ready, p_turned, p_copied, p_used, o_done, pair_done, stored, o_free = (
            sem(n) for n in ("max_ready", "p_ready", "p_turned", "p_copied", "p_used", "o_done", "pair_done", "stored", "o_free"))
        PGROUPS = NP // G + 1 + WP // G + 1
        with nc.Block() as block:

            @block.sync
            def _(sp):
                for a, src in enumerate((z, qk)):
                    for h in range(KVH):
                        sp.dma_start(qn[:, a, :, h], src[row, h * GC * DC:(h + 1) * GC * DC].rearrange("t (g d) -> t g d", d=DC)).then_inc(small_loaded, 16)
                sp.dma_start(kn[:].rearrange("t a c -> t (a c)"), qk[row, CQ:CQ + 2 * KVW]).then_inc(small_loaded, 16)
                sp.dma_start(vn[:, 0], z[row, OFF_SEL + KVW:OFF_SEL + 2 * KVW]).then_inc(small_loaded, 16)
                sp.dma_start(vn[:, 1], z[row, OFF_WIN + KVW:OFF_WIN + 2 * KVW]).then_inc(small_loaded, 16)
                with sp.Fori(0, PAIRS // 2) as i:
                    for j in range(2):
                        u = 2 * i + j
                        sp.wait_ge(pair_done, u + 1)
                        for b in range(2):
                            sp.dma_start(kv[:, j, NP:STEPS, b], win[bass.ds(2 * u + b, 1)].rearrange("o (a p) c -> p (o a) c", p=P)).then_inc(loaded[j], 16)
                            with sp.Fori(0, NP) as a:
                                page = sp.value_load(pages[0:1, bass.ds((2 * u + b) * NP + a, 1)], min_val=0, max_val=sel_pool.shape[0] - 1)
                                sp.dma_start(kv[:, j, bass.ds(a, 1), b].rearrange("p a c -> p (a c)"),
                                             sel_pool[bass.ds(page, 1)].rearrange("o p c -> p (o c)")).then_inc(loaded[j], 16)

            @block.tensor
            def _(pe):
                T, M = nc.tensor.transpose, nc.tensor.matmul
                pe.wait_ge(small_loaded, 112)
                for a in range(2):
                    for g in range(GC):
                        T(psS[:, a, g * NS:(g + 1) * NS], qn[:, a, g].rearrange("t h d -> t (h d)"), ident[0:NS, 0:NS])
                    last = T(psM[:, a * NS:(a + 1) * NS], kn[:, a], ident[0:NS, 0:NS])
                last.then_inc(n_turned, 1)
                pe.wait_ge(n_copied, 1)

                def pair(i, j):
                    u = 2 * i + j
                    pe.wait_ge(qp_ready, u + 1)
                    for q in range(Q4):
                        last = M(psM[32 * q:32 * q + 32, 0:NCMP_S], qp[:, 0, q // 2, q % 2], kcp[:, q // 2, 0:NCMP_S], start=True, stop=True)
                    last.then_inc(c_scored, 1)
                    pe.wait_ge(c_norm, u + 1)
                    T(psM[0:NCMP_S, 128:256], sc[:, 0:NCMP_S], ident).then_inc(c_turned, 1)
                    pe.wait_ge(c_copied, u + 1)
                    M(psM[:, 256:256 + NSLC], pcT[0:NCMP_S, :], wslc, start=True, stop=True).then_inc(imp1, 1)
                    pe.wait_ge(imp1_read, u + 1)
                    M(psM[:, 320:320 + NSLC], gsum, imp[:], start=True, stop=True).then_inc(imp2, 1)
                    for br in range(2):
                        for q in range(Q4):
                            last = M(psP[32 * q:32 * q + 32, 1, 32 * br:32 * br + NS], qp[:, 1, q // 2, q % 2], KN[:, br], start=True, stop=True)
                    last.then_inc(new_scored, 1)
                    pe.wait_ge(loaded[j], (i + 1) * (2 * (NP + 1) * 16))

                    def keys(n):
                        pe.wait_ge(k_copied, u * STEPS + n + 1)
                        for b in range(2):
                            last = T(psK[:, n % 2, b], kv[:, j, n, b, 0:KVW], ident)
                        last.then_inc(k_turned, 1)

                    def scores(n):
                        g = n // G
                        pe.wait_ge(k_copied, u * STEPS + n + 3)
                        if n % G == 0:
                            pe.wait_ge(group_read, u * NG + g + 1)
                        for q in range(Q4):
                            last = M(psS[32 * q:32 * q + 32, g % 2, (n % G) * P:(n % G + 1) * P], qp[:, 1, q // 2, q % 2], kT[:, n % 2, q // 2], start=True, stop=True)
                        last.then_inc(page_scored, 1)

                    keys(0)
                    for n in range(1, STEPS):
                        keys(n)
                        scores(n - 1)
                    scores(STEPS - 1)
                    for b in range(2):
                        M(psO[64 * b:64 * b + 64, 0], pcT[0:NCMP_S, 64 * b:64 * b + 64], vcp[0:NCMP_S, b], start=True, stop=True)
                    pe.wait_ge(p_ready, u + 1)
                    groups = [[("s", g * G + c) for c in range(G)] for g in range(NP // G)] + [[("n", 0)]]
                    groups += [[("w", c) for c in range(WP)], [("n", 1)]]

                    def turn(k):
                        if k >= 2:
                            pe.wait_ge(p_copied, u * PGROUPS + k - 1)
                        for c, (kind, a) in enumerate(groups[k]):
                            if kind == "n":
                                src = (ss[:, PAST:S2], sw[:, WIN:W2])[a]
                                last = T(psP[0:NS, k % 2, 0:P], src, ident)
                            else:
                                last = T(psP[:, k % 2, c * P:(c + 1) * P], (ss if kind == "s" else sw)[:, a * P:(a + 1) * P], ident)
                        last.then_inc(p_turned, 1)

                    def product(k):
                        pe.wait_ge(p_copied, u * PGROUPS + k + 1)
                        for c, (kind, a) in enumerate(groups[k]):
                            for b in range(2):
                                r = slice(64 * b, 64 * b + 64)
                                if kind == "n":
                                    last = M(psO[r, 1 + a], pT[0:NS, k % 2, 0, r], vn[:, a], start=False, stop=True)
                                else:
                                    page = a if kind == "s" else NP + a
                                    last = M(psO[r, 1 if kind == "s" else 2], pT[:, k % 2, c, r], kv[:, j, page, b, KVW:2 * KVW], start=a == 0, stop=False)
                        last.then_inc(p_used, 1)

                    for k in range(PGROUPS):
                        turn(k)
                        if k:
                            product(k - 1)
                    product(PGROUPS - 1)
                    nc.tensor.drain().then_inc(o_done, 1)
                    pe.wait_ge(pair_done, u + 3)

                with pe.Fori(0, PAIRS // 2) as i:
                    for j in range(2):
                        pair(i, j)

            @block.scalar
            def _(act):
                a = nc.scalar
                act.wait_ge(n_copied, 1)
                with act.Fori(0, PAIRS // 2) as i:
                    for j in range(2):
                        u = 2 * i + j
                        act.wait_ge(c_max, u + 1)
                        a.activation(sc[:, 0:NCMP_S], psM[:, 0:NCMP_S], ACT.Exp, scale=SC, bias=nm[:, 0:1], accum_out=l[:, 0:1])
                        a.drain().then_inc(c_exp, 1)
                        for n in range(STEPS):
                            act.wait_ge(k_turned, u * STEPS + n + 1)
                            act.wait_ge(page_scored, u * STEPS + n + 1)
                            a.activation(kT[:, n % 2], psK[:, n % 2, 0:2], ACT.Copy).then_inc(k_copied, 1)
                        act.wait_ge(max_ready, u + 1)
                        a.activation(ss[:], ss[:], ACT.Exp, scale=SC, bias=nm[:, 1:2], accum_out=l[:, 1:2])
                        a.activation(sw[:], sw[:], ACT.Exp, scale=SC, bias=nm[:, 2:3], accum_out=l[:, 2:3])
                        a.drain().then_inc(p_ready, 1)

            @block.vector
            def _(dve):
                v = nc.vector
                dve.sem_inc(pair_done, 2)
                dve.sem_inc(k_copied, 2)
                dve.sem_inc(page_scored, 2)
                dve.sem_inc(group_read, 2)
                dve.wait_ge(n_turned, 1)
                for k in range(2):
                    v.tensor_copy(QT[:, k].rearrange("p b (g t) -> p b g t", t=DEC_T),
                                  psS[:, k, 0:GC * NS].rearrange("p (g b t) -> p b g t", g=GC, t=DEC_T))
                v.tensor_copy(KN[:].rearrange("p a t -> p (a t)"), psM[:, 0:2 * NS])
                v.memset(qp[:], 0.0)
                v.drain().then_inc(n_copied, 1)

                def pair(i, j):
                    u = 2 * i + j
                    two = bass.ds(2 * u, 2)
                    for h in range(KVH):
                        d = slice(h * DC, (h + 1) * DC)
                        v.tensor_copy(qp[d, :, :, h], QT[d, :, two])
                    v.tensor_copy(kcp[:, :, 0:NCMP_S], KC[:, two, 0:NCMP_S])
                    v.tensor_copy(vcp[0:NCMP_S], VC[0:NCMP_S, two])
                    v.drain().then_inc(qp_ready, 1)
                    dve.wait_ge(c_scored, u + 1)
                    v.reduce_max(mx[:, 0:1], psM[:, 0:NCMP_S], AX.X)
                    v.drain()
                    v.tensor_scalar_mul(nm[:, 0:1], mx[:, 0:1], -SC).then_inc(c_max, 1)
                    dve.wait_ge(c_exp, u + 1)
                    v.tensor_scalar_max(rl[:, 0:1], l[:, 0:1], 1e-30)
                    v.drain()
                    v.reciprocal(rl[:, 0:1], rl[:, 0:1])
                    v.drain()
                    v.tensor_scalar(sc[:, 0:NCMP_S], sc[:, 0:NCMP_S], rl[:, 0:1], None, ALU.mult).then_inc(c_norm, 1)
                    dve.wait_ge(c_turned, u + 1)
                    v.tensor_copy(pcT[0:NCMP_S, :], psM[0:NCMP_S, 128:256]).then_inc(c_copied, 1)
                    dve.wait_ge(imp1, u + 1)
                    v.tensor_copy(imp[:], psM[:, 256:256 + NSLC]).then_inc(imp1_read, 1)
                    dve.wait_ge(imp2, u + 1)
                    v.tensor_tensor(x1[:], psM[:, 320:320 + NSLC], forced, ALU.add)
                    for src, dst in ((x1, x2), (x2, x1)):
                        v.drain()
                        v.max(m8[:], src[:])
                        v.drain()
                        v.match_replace(dst[:], m8[:], src[:], NEG)
                    v.drain()
                    v.tensor_scalar(x1[:], x1[:], NEG / 2, NEG, ALU.is_gt, ALU.mult)
                    v.drain()
                    dve.wait_ge(new_scored, u + 1)
                    v.tensor_tensor(ss[:, PAST:S2], psP[:, 1, 0:NS], new_mask[:, 0, bass.ds(u, 1)].rearrange("p o t -> p (o t)"), ALU.add)
                    v.tensor_tensor(sw[:, WIN:W2], psP[:, 1, NS:2 * NS], new_mask[:, 1, bass.ds(u, 1)].rearrange("p o t -> p (o t)"), ALU.add)
                    nb = G * PAGE // SBLK
                    for g in range(NG):
                        dve.wait_ge(page_scored, u * STEPS + (g + 1) * G + 2)
                        if g < NP // G:
                            v.tensor_tensor(ss[:, g * 512:(g + 1) * 512].rearrange("p (n k) -> p n k", k=SBLK),
                                            psS[:, g % 2].rearrange("p (n k) -> p n k", k=SBLK),
                                            x1[:, g * nb:(g + 1) * nb].unsqueeze(2).to_broadcast([P, nb, SBLK]), ALU.add)
                        else:
                            v.tensor_tensor(sw[:, 0:WIN], psS[:, g % 2], win_mask, ALU.add)
                        v.drain().then_inc(group_read, 1)
                    v.reduce_max(mx[:, 1:2], ss[:], AX.X)
                    v.reduce_max(mx[:, 2:3], sw[:], AX.X)
                    v.drain()
                    v.tensor_scalar_mul(nm[:, 1:3], mx[:, 1:3], -SC).then_inc(max_ready, 1)
                    for k in range(PGROUPS):
                        dve.wait_ge(p_turned, u * PGROUPS + k + 1)
                        if k >= 2:
                            dve.wait_ge(p_used, u * PGROUPS + k - 1)
                        if k == NP // G or k == PGROUPS - 1:
                            v.tensor_copy(pT[0:NS, k % 2, 0], psP[0:NS, k % 2, 0:P]).then_inc(p_copied, 1)
                        else:
                            v.tensor_copy(pT[:, k % 2].rearrange("p c r -> p (c r)"), psP[:, k % 2]).then_inc(p_copied, 1)
                    v.tensor_copy(w[:, 0:1], gates[:, bass.ds(u, 1), 0])
                    v.reciprocal(rl[:, 1:3], l[:, 1:3])
                    v.drain()
                    v.tensor_tensor(w[:, 1:3], rl[:, 1:3], gates[:, bass.ds(u, 1), 1:3].rearrange("p o b -> p (o b)"), ALU.mult)
                    v.drain()
                    dve.wait_ge(o_done, u + 1)
                    for q in range(Q4):
                        r = slice(32 * q, 32 * q + 32)
                        v.tensor_tensor(o3[r], psO[r, :, (q % 2) * DC:(q % 2 + 1) * DC], w[r].unsqueeze(2).to_broadcast([32, 3, DC]), ALU.mult)
                    v.drain()
                    v.reduce_sum(o[:, j], o3[:].rearrange("p b d -> p d b"), AX.X)
                    v.drain().then_inc(pair_done, 1)

                with dve.Fori(0, PAIRS // 2) as i:
                    for j in range(2):
                        if j == 0:
                            dve.wait_ge(o_free, i + 1)
                        pair(i, j)

            @block.gpsimd
            def _(pool):
                pool.sem_inc(o_free, 1)
                with pool.Fori(0, PAIRS // 2) as i:
                    pool.wait_ge(pair_done, 2 * i + 4)
                    for j in range(2):
                        pool.dma_start(out[bass.ds((2 * i + j) * P, P), :], o[:, j]).then_inc(stored, 16)
                    pool.wait_ge(stored, 32 * i + 32)
                    pool.sem_inc(o_free, 1)


def shape_constants():
    f = np.float32
    neg, big = f(-1e30), f(1e30)
    p, half = 128, 32
    c = {"ident": np.eye(p, dtype=f), "zeros": np.zeros((96, 1024), f)}
    pos = np.concatenate([np.arange(1024), np.tile(2048 + np.arange(4), 8), np.zeros(96)]).astype(f)
    inv = (f(1.0) / (f(10000.0) ** (np.arange(half, dtype=f) / f(half)))).astype(f)
    ang = pos[:, None] * inv[None, :]
    c["cos"], c["sin"] = np.cos(ang).astype(f), np.sin(ang).astype(f)
    q, k = np.arange(p)[:, None], np.arange(p)[None]
    m = np.full((3, 8, p, 2 * p), neg, f)
    for i in range(8):
        for g in range(3):
            m[g, i, :, p:][(q >= k) & ((g < 2) | (q // 64 == k // 64))] = 0
            if (g == 0 and i > 0) or (g == 1 and i % 2):
                m[g, i, :, :p][k >= q] = 0
    c["mask_a"] = m.reshape(-1, 2 * p)
    t, tok = np.arange(p) % 4, np.arange(p) % 32
    new = np.arange(32)
    m = np.full((p, 3, p + 32), neg, f)
    m[:, 0, :p][np.arange(p)[None] >= t[:, None]] = 0
    m[:, 1:, :p] = 0
    same = tok[:, None] // 4 == new[None] // 4
    m[:, 0, p:][same & (new[None] <= tok[:, None])] = 0
    for g in (1, 2):
        m[:, g, p:][new[None] == tok[:, None]] = 0
    c["mask_as"] = m
    c["rowsel"] = np.repeat(np.eye(4, dtype=f)[:, :, None], p, 2)
    c["later"] = np.where(q > k, big, f(0))
    s = np.arange(32)
    mine = s[:, None] // 4 == s[None] // 4
    c["later_s"] = np.where(mine & (s[:, None] <= s[None]), f(0), big)
    c["own"] = (s[:, None] // 4 == np.arange(8)[None]).astype(f)
    c["own_cols"] = np.broadcast_to(c["own"].T[None], (p, 8, 32)).copy()
    return c


def nsa_constants():
    f, neg = np.float32, np.float32(-1e30)
    p = 128
    c = {}
    q, k = np.arange(p)[:, None], np.arange(p)[None]
    c["causal"] = np.where(k <= q, f(0), neg)
    c["early"] = np.where(k > q, f(0), neg)
    t = np.arange(1024).reshape(8, p).T[:, :, None]
    c["mask_c"] = np.where(16 * np.arange(63)[None, None] + 31 <= t, f(0), neg)
    n, j = np.arange(127)[:, None], np.arange(33)[None]
    c["wslc"] = ((n >= 4 * j - 1) & (n <= 4 * j + 3)).astype(f)
    r = np.arange(p)
    c["gsum"] = ((r[:, None] // 32 == r[None] // 32) & (r[:, None] % 4 == r[None] % 4)).astype(f)
    c["forced"] = np.broadcast_to(np.where((j == 0) | (j == 32) | (j == 31), f(1e30), f(0)), (p, 33)).astype(f)
    pair, tok = np.arange(4)[None, :, None], np.arange(32)[None, None]
    b, t = r[:, None, None] // 64, r[:, None, None] % 4
    ok = (tok // 4 == 2 * pair + b) & (tok % 4 <= t)
    c["new_mask"] = np.repeat(np.where(ok, f(0), neg)[:, None], 2, 1)
    c["win_mask"] = np.where(np.arange(512)[None] > (r % 4)[:, None], f(0), neg)
    return c


IN_SHAPES = ("x_prompt", "x_sample", "cache_a0_kv", "cache_a1_kv", "cache_a2_kv", "state_b_C", "state_b_n", "state_b_m",
             "cache_c_cmp_kv", "cache_c_sel_kv", "cache_c_win_kv", "page_table", "norm_g", "w_in_ab", "b_if", "g_mlstm",
             "w_out_ab", "w_in_c", "cmp_w1", "cmp_w2", "cmp_pe", "w_out_c", "w_ffn_gate", "w_ffn_up", "w_ffn_down", "norm_final")
CONSTANTS = ("zeros", "ident", "cos", "sin", "mask_a", "mask_as", "rowsel", "later", "later_s", "own", "own_cols", "causal", "early",
             "mask_c", "wslc", "gsum", "forced", "new_mask", "win_mask")
OUT_SHAPES = (
    (1, SEQ, D), (DEC_B, DEC_T, D),
    (1, 1, 128, 2, HA, DA), (1, DEC_B, 128, 2, HA, DA), (1, 1, 512, 2, HA, DA), (1, DEC_B, 512, 2, HA, DA),
    (1, 1, SEQ, 2, HA, DA), (1, DEC_B, PAST, 2, HA, DA),
    (1, 1, HB, DB, DB), (1, DEC_B, HB, DB, DB), (1, 1, HB, DB), (1, DEC_B, HB, DB), (1, 1, HB), (1, DEC_B, HB),
    (1, 1, SEQ, 2, KVH, DC), (1, DEC_B, DEC_T, 2, KVH, DC), (1, 1, SEQ, 2, KVH, DC), (1, DEC_B, DEC_T, 2, KVH, DC),
    (1, 1, WIN, 2, KVH, DC), (1, DEC_B, WIN, 2, KVH, DC))


def build(nc, i, c, o):
    (y_p, y_s, a0_p, a0_s, a1_p, a1_s, a2_p, a2_s, bC_p, bC_s, bn_p, bn_s, bm_p, bm_s,
     ccmp_p, ccmp_s, csel_p, csel_s, cwin_p, cwin_s) = o
    Sems.used.clear()
    scratch = lambda name, shape: nc.dram_tensor(name, shape, F32, kind="Internal").ap()
    hid = [scratch(f"hidden{k}", (ROWS, D)) for k in range(5)]
    z_ab, qk_ab = scratch("z_ab", (ROWS, IN_AB)), scratch("qk_ab", (ROWS, 2 * QA))
    q_res, kv_res = scratch("q_res", (GA * SEQ, AW)), scratch("kv_res", (P + GA * SEQ, 2 * AW))
    OW = HA * (DA + 1)
    o_res = scratch("o_res", (GA * SEQ, OW))
    o_dil = [scratch(f"o_dil{g}", (ROWS, OW)) for g in range(GA)]
    h_b, mixed = scratch("h_b", (ROWS, BW)), scratch("mixed", (ROWS, MIX))
    z_c, qk_c = scratch("z_c", (ROWS, IN_C)), scratch("qk_c", (ROWS, CQ + 2 * KVW))
    gate_rows, o_rows, o_c = scratch("gate_rows", (DEC_B * HC * DEC_T, 3)), scratch("o_rows", (DEC_B * HC * DEC_T, DC)), scratch("o_c", (ROWS, CQ))
    caches = [i[f"cache_a{g}_kv"][0].rearrange("b w a h d -> b w (a h d)") for g in range(GA)]
    a_s = [x[0].rearrange("b w a h d -> b w (a h d)") for x in (a0_s, a1_s, a2_s)]
    a_p = [x[0, 0].rearrange("w a h d -> w (a h d)") for x in (a0_p, a1_p, a2_p)]
    win_in = i["cache_c_win_kv"][0].rearrange("b w a h d -> b w (a h d)")
    win_out = cwin_s[0].rearrange("b w a h d -> b w (a h d)")
    flat_c = lambda x: x.rearrange("o b t a h d -> (o b t) (a h d)")
    pad = slice(TOK, ROWS)
    sam, pro = slice(SEQ, TOK), slice(0, SEQ)

    with ExitStack() as ctx:
        sb = lambda n, s, t=F32: ctx.enter_context(nc.sbuf_tensor(n, s, t))[:]
        k = {}
        src, dst = [], []

        def resident(name, ap, shape, t=F32):
            k[name] = sb(f"c_{name}", shape, t)
            src.append(ap)
            dst.append(k[name])

        for name in ("ident", "rowsel", "later", "later_s", "own", "own_cols", "causal", "early", "mask_c", "wslc", "gsum", "forced",
                     "new_mask", "win_mask"):
            resident(name, c[name], list(c[name].shape))
        for layer in range(2):
            for m in range(2):
                resident(f"gain{layer}{m}", i["norm_g"][layer, m].rearrange("(k p) -> p k", p=P), [P, KD])
        resident("gain_b", i["g_mlstm"].to_broadcast([P, BW]), [P, BW])
        resident("pages", i["page_table"], [1, DEC_B * PAST // PAGE], I32)

        kept = ctx.enter_context(nc.semaphore("kept_rows_copied"))
        keep = [(a_s[g], caches[g], w) for g, w in enumerate((128, 512, PAST))] + [(win_out, win_in, WIN)]
        N_C, TURN = 460, 2
        SEQS = DEC_B * N_C * TURN // IN_C
        assert SEQS * IN_C == DEC_B * N_C * TURN

        def keep_rows(eng, i):
            for n in range(SEQS):
                b = bass.ds(i * SEQS + n, 1)
                for to, of, w in keep:
                    eng.dma_start(to[b, 0:w - DEC_T], of[b, DEC_T:w]).then_inc(kept, 16)

        load_constants(nc, "constants", src, dst)
        copy_rows(nc, "hidden_in", [(hid[0][pro], i["x_prompt"][0]), (hid[0][sam], i["x_sample"].rearrange("b t d -> (b t) d")),
                                    (hid[0][pad], c["zeros"])])

        def mixer_in(tag, h, gain, w, out, n, meanwhile=None):
            with nc.sbuf_tensor(f"{tag}_x_hi", [P, KD, ROWS], FR) as hi, nc.sbuf_tensor(f"{tag}_x_lo", [P, KD, ROWS], FR) as lo:
                norm_transpose(nc, f"{tag}_norm", h, gain, k["ident"], hi[:], lo[:])
                project(nc, f"{tag}_in", hi[:], KD, w, out, n, meanwhile=meanwhile, lo=lo[:])

        def mixer_out(tag, x, kc, w, h, out):
            with nc.sbuf_tensor(f"{tag}_m_hi", [P, kc, ROWS], FR) as hi, nc.sbuf_tensor(f"{tag}_m_lo", [P, kc, ROWS], FR) as lo:
                transpose_rows(nc, f"{tag}_turn", x, kc, k["ident"], hi[:], lo[:])
                project(nc, f"{tag}_out", hi[:], kc, w, out, 256, resid=h, lo=lo[:])

        def ffn(tag, layer, h, out):
            with nc.sbuf_tensor(f"{tag}_hT", [P, KF, ROWS], F32) as hT:
                with nc.sbuf_tensor(f"{tag}_x_hi", [P, KD, ROWS], FR) as hi, nc.sbuf_tensor(f"{tag}_x_lo", [P, KD, ROWS], FR) as lo:
                    norm_transpose(nc, f"{tag}_norm", h, k[f"gain{layer}1"], k["ident"], hi[:], lo[:], spare=hT[:])
                    ffn_hidden(nc, f"{tag}_hid", hi[:], lo[:], i["w_ffn_gate"][layer], i["w_ffn_up"][layer], hT[:])
                project(nc, f"{tag}_down", hT[:], KF, i["w_ffn_down"][layer], out, 256, resid=h)

        mixer_in("ab", hid[0], k["gain00"], i["w_in_ab"][0], z_ab, 436)
        rope(nc, "rope_a", z_ab, ((0, 2 * GA * HA),), c["cos"], c["sin"], qk_ab)
        moves = [(kv_res[0:P, 0:AW], qk_ab[0:P, QA:QA + AW]), (kv_res[0:P, AW:2 * AW], z_ab[0:P, OFF_VA:OFF_VA + AW]),
                 (h_b[pad], z_ab[pad, OFF_QB:OFF_QB + BW])]
        final = []
        for g, (win, dil) in enumerate(DIL):
            col = lambda at: slice(at + g * AW, at + (g + 1) * AW)
            by_residue = lambda ap: ap.rearrange("(m r) c -> r m c", r=dil)
            grouped = lambda ap: ap.rearrange("(r m) c -> r m c", r=dil)
            kv_g = kv_res[P + g * SEQ:P + (g + 1) * SEQ]
            moves += [(grouped(q_res[g * SEQ:(g + 1) * SEQ]), by_residue(qk_ab[pro, col(0)])),
                      (grouped(kv_g[:, 0:AW]), by_residue(qk_ab[pro, col(QA)])),
                      (grouped(kv_g[:, AW:2 * AW]), by_residue(z_ab[pro, col(OFF_VA)]))]
            w_p, w_s = min(win, SEQ), min(win, PAST)
            final += [(a_p[g][:, 0:AW], qk_ab[SEQ - w_p:SEQ, col(QA)]), (a_p[g][:, AW:2 * AW], z_ab[SEQ - w_p:SEQ, col(OFF_VA)]),
                      (a_s[g][:, w_s - DEC_T:w_s, 0:AW], qk_ab[sam, col(QA)].rearrange("(b t) c -> b t c", t=DEC_T)),
                      (a_s[g][:, w_s - DEC_T:w_s, AW:2 * AW], z_ab[sam, col(OFF_VA)].rearrange("(b t) c -> b t c", t=DEC_T))]
            moves.append((o_dil[g][pad], z_ab[pad, 0:OW]))
        copy_rows(nc, "regroup", moves, final, kept)
        dilated_prompt(nc, "dil_p", q_res, kv_res, c["mask_a"], k["ident"], o_res)
        recycle(nc)
        dilated_sample(nc, "dil_s", qk_ab, z_ab, caches, c["mask_as"], k["ident"], o_dil)
        with ExitStack() as gates_ctx:
            sg = lambda n, s: gates_ctx.enter_context(nc.sbuf_tensor(n, s, F32))[:]
            Mrow, cols, dec = sg("Mrow", [HB, TOK]), sg("cols", [P, TILES, 4, HB]), sg("dec", [P, PT, HB])
            dec_s, dec_sT = sg("dec_s", [P, HB, DEC_B]), sg("dec_sT", [DEC_B, HB])
            mlstm_gates(nc, "gates_b", z_ab, i["b_if"][0], i["state_b_m"][0], k["ident"], Mrow, cols, dec, dec_s, dec_sT, bm_p[0], bm_s[0])
            mlstm_prompt(nc, "mlstm_p", z_ab, Mrow, cols, dec, k["rowsel"], k["later"], k["ident"], h_b, bC_p[0, 0], bn_p[0, 0])
            mlstm_sample(nc, "mlstm_s", z_ab, Mrow, cols, dec_s, dec_sT, k["rowsel"], k["later_s"], k["own"], k["own_cols"],
                         i["state_b_C"][0], i["state_b_n"][0], k["ident"], h_b, bC_s[0], bn_s[0])
        copy_rows(nc, "ungroup", [(o_dil[g][pro].rearrange("(m r) c -> r m c", r=dil),
                                   o_res[g * SEQ:(g + 1) * SEQ].rearrange("(r m) c -> r m c", r=dil)) for g, (_, dil) in enumerate(DIL)])
        recycle(nc)
        merge_heads(nc, "merge", o_dil, h_b, z_ab, k["gain_b"], mixed)
        mixer_out("ab", mixed, MIX // P, i["w_out_ab"][0], hid[0], hid[1])
        ffn("ffn0", 0, hid[1], hid[2])
        recycle(nc)

        mixer_in("c", hid[2], k["gain10"], i["w_in_c"][0], z_c, N_C, keep_rows)
        rope(nc, "rope_c", z_c, ((0, HC), (OFF_SEL, KVH), (OFF_WIN, KVH)), c["cos"], c["sin"], qk_c)
        per_seq = lambda ap: ap.rearrange("(b t) c -> b t c", t=DEC_T)
        heads = lambda ap, n: ap.rearrange("t (h d) -> h t d", d=n)
        moves = [(o_c[pad], c["zeros"])]
        final_c = [(flat_c(ccmp_p), z_c[pro, OFF_CMP:OFF_CMP + 2 * KVW]), (flat_c(ccmp_s), z_c[sam, OFF_CMP:OFF_CMP + 2 * KVW])]
        for rows, sel in ((pro, csel_p), (sam, csel_s)):
            final_c += [(flat_c(sel)[:, 0:KVW], qk_c[rows, CQ:CQ + KVW]), (flat_c(sel)[:, KVW:2 * KVW], z_c[rows, OFF_SEL + KVW:OFF_SEL + 2 * KVW])]
        final_c += [(flat_c(cwin_p)[:, 0:KVW], qk_c[SEQ - WIN:SEQ, CQ + KVW:CQ + 2 * KVW]),
                  (flat_c(cwin_p)[:, KVW:2 * KVW], z_c[SEQ - WIN:SEQ, OFF_WIN + KVW:OFF_WIN + 2 * KVW]),
                  (win_out[:, WIN - DEC_T:WIN, 0:KVW], per_seq(qk_c[sam, CQ + KVW:CQ + 2 * KVW])),
                  (win_out[:, WIN - DEC_T:WIN, KVW:2 * KVW], per_seq(z_c[sam, OFF_WIN + KVW:OFF_WIN + 2 * KVW]))]
        per_b = HC * DEC_T
        for b in range(DEC_B):
            moves.append((gate_rows[b * per_b:(b + 1) * per_b].rearrange("(h t) c -> h t c", t=DEC_T),
                          heads(z_c[SEQ + b * DEC_T:SEQ + (b + 1) * DEC_T, OFF_GATE:IN_C], 3)))
        copy_rows(nc, "new_rows", moves, final_c, kept)
        recycle(nc)
        with ExitStack() as c_ctx:
            sc = lambda n, s: c_ctx.enter_context(nc.sbuf_tensor(n, s, F32))[:]
            KC, KP, VC = sc("KC", [P, DEC_B, P]), sc("KP", [P, KVH, NCMP_P + 1]), sc("VC", [P, DEC_B + 1, KVW])
            gp, gs = sc("gates_p", [P, PT, HC * 3]), sc("gates_s", [P, DEC_B // 2, 3])
            compress(nc, "cmp", i["cache_c_cmp_kv"][0].rearrange("n p a h d -> n p (a h d)"), k["pages"], z_c, i["cmp_w1"][0], i["cmp_w2"][0],
                     i["cmp_pe"][0], k["ident"], KC, KP, VC)
            gate_sigmoid(nc, "gate_p", z_c[pro, OFF_GATE:IN_C].rearrange("(a p) c -> p a c", p=P), gp)
            gate_sigmoid(nc, "gate_s", gate_rows.rearrange("(a p) c -> p a c", p=P), gs)
            recycle(nc)
            nsa_prompt(nc, "nsa_p", z_c, qk_c, k["mask_c"], k["causal"], k["early"], KP, VC, gp.rearrange("p i (h b) -> p i h b", b=3),
                       k["ident"], o_c)
            recycle(nc)
            nsa_sample(nc, "nsa_s", z_c, qk_c, i["cache_c_sel_kv"][0].rearrange("n p a h d -> n p (a h d)"), k["pages"], win_in, KC, VC, gs,
                       k["wslc"], k["gsum"], k["forced"], k["new_mask"], k["win_mask"], k["ident"], o_rows)
        copy_rows(nc, "sample_rows", [(heads(o_c[SEQ + b * DEC_T:SEQ + (b + 1) * DEC_T], DC),
                                       o_rows[b * per_b:(b + 1) * per_b].rearrange("(h t) d -> h t d", t=DEC_T)) for b in range(DEC_B)])
        recycle(nc)
        mixer_out("c", o_c, KD, i["w_out_c"][0], hid[2], hid[3])
        ffn("ffn1", 1, hid[3], hid[4])
        gain_f = sb("c_gain_f", [P, D])
        load_constants(nc, "gain_final", [i["norm_final"].unsqueeze(0).to_broadcast([P, D])], [gain_f])
        final_norm(nc, "final", hid[4], gain_f, y_p[0], y_s.rearrange("b t d -> (b t) d"))
        with nc.Block() as block:

            @block.sync
            def _(sp):
                sp.wait_ge(kept, 16 * (len(keep) * DEC_B + len(final) + len(final_c)))


def kernel(**inputs):
    from concourse import bacc
    from concourse.bass_utils import run_bass_kernel_spmd

    nc = bacc.Bacc("TRN2", target_bir_lowering=False, num_devices=1)
    arrays, ins, cs = {}, {}, {}

    def given(name, a):
        arrays[name] = a
        return nc.dram_tensor(name, a.shape, mybir.dt.from_np(a.dtype), kind="ExternalInput").ap()

    for name in IN_SHAPES:
        a = np.ascontiguousarray(inputs[name])
        ins[name] = given(f"in_{name}", a.reshape(1, -1) if name == "page_table" else a)
    for name, a in {**shape_constants(), **nsa_constants()}.items():
        cs[name] = given(f"const_{name}", np.ascontiguousarray(a))
    outs = [nc.dram_tensor(f"out_{n}", s, F32, kind="ExternalOutput").ap() for n, s in enumerate(OUT_SHAPES)]
    build(nc, ins, cs, outs)
    r = run_bass_kernel_spmd(nc, [arrays], core_ids=[0])
    return tuple(r.results[0][f"out_{n}"] for n in range(len(OUT_SHAPES)))
```
